# Optimizing a Trainium2 kernel written in Bass

```python
import jax
import jax.numpy as jnp
from jax import lax
import numpy as np
import math
import jax, jax.numpy as jnp

D_MODEL = 1024
BATCH = 1
SEQ = 256
DEPTH = 1

GRID_W = 64
CTX_LEN = 256
NA_HEAD_DIM = 64
N_NA_HEADS = (D_MODEL // 2) // NA_HEAD_DIM
NA_WIDTH = N_NA_HEADS * NA_HEAD_DIM
NA_WIN_H = 8
NA_WIN_W = 16
NA_QBLOCK_W = 16
NA_KSPAN_W = NA_QBLOCK_W + NA_WIN_W
ROPE_BASE = 10000.0
HG_DK = 128
HG_DV = 128
N_HG_HEADS = (D_MODEL // 2) // HG_DV
HG_KEY_WIDTH = N_HG_HEADS * HG_DK
HG_WIDTH = N_HG_HEADS * HG_DV
HG_CHUNK = 32
MIX_WIDTH = NA_WIDTH + HG_WIDTH
IN_COLS = 3 * NA_WIDTH + 3 * HG_KEY_WIDTH + 2 * HG_WIDTH
N_EXPERTS = 16
EC_CAPACITY_FACTOR = 2
D_EXPERT = ((8 * D_MODEL // 3 + 63) // 64) * 64
RMS_EPS = 1e-6


def rms_norm(x, g):
    xf = x.astype(jnp.float32)
    y = xf * lax.rsqrt(jnp.mean(xf * xf, axis=-1, keepdims=True) + RMS_EPS)
    return (y * g.astype(jnp.float32)).astype(x.dtype)

def modulate(h, shift, scale):
    return h * (1.0 + scale) + shift

def to_heads(x, n_heads):
    b, t, w = x.shape
    return x.reshape(b, t, n_heads, w // n_heads).transpose(0, 2, 1, 3)

def from_heads(x):
    b, h, t, d = x.shape
    return x.transpose(0, 2, 1, 3).reshape(b, t, h * d)

def split_cols(p):
    sizes = (NA_WIDTH, NA_WIDTH, NA_WIDTH, HG_KEY_WIDTH, HG_KEY_WIDTH, HG_KEY_WIDTH, HG_WIDTH, HG_WIDTH)
    bounds = []
    acc = 0
    for s in sizes[:-1]:
        acc += s
        bounds.append(acc)
    return jnp.split(p, bounds, axis=-1)

def rope_1d(x, pos):
    d = x.shape[-1]
    inv_freq = ROPE_BASE ** (-jnp.arange(0, d, 2, dtype=jnp.float32) / d)
    ang = pos[:, None] * inv_freq[None, :]
    cos = jnp.cos(ang).astype(x.dtype)
    sin = jnp.sin(ang).astype(x.dtype)
    x1, x2 = x[..., : d // 2], x[..., d // 2:]
    return jnp.concatenate([x1 * cos - x2 * sin, x1 * sin + x2 * cos], axis=-1)

def axial_rope(x, row_pos, col_pos):
    half = x.shape[-1] // 2
    return jnp.concatenate([rope_1d(x[..., :half], row_pos), rope_1d(x[..., half:], col_pos)], axis=-1)

def neighbourhood_attention(q, k, v, k_ctx, v_ctx, rpb):
    bsz, nh, seq, dh = q.shape
    rows = seq // GRID_W
    kh = min(NA_WIN_H, rows)
    ncb = GRID_W // NA_QBLOCK_W
    scale = dh ** -0.5
    t = jnp.arange(seq)
    row_pos = (t // GRID_W).astype(jnp.float32)
    col_pos = (t % GRID_W).astype(jnp.float32)
    q_rot = axial_rope(q, row_pos, col_pos)
    k_rot = axial_rope(k, row_pos, col_pos)
    r = jnp.arange(rows)
    r0 = jnp.clip(r - kh // 2, 0, rows - kh)
    key_rows = r0[:, None] + jnp.arange(kh)[None, :]
    j = jnp.arange(ncb)
    c0 = jnp.clip(j * NA_QBLOCK_W - NA_WIN_W // 2, 0, GRID_W - NA_KSPAN_W)
    key_cols = c0[:, None] + jnp.arange(NA_KSPAN_W)[None, :]
    tok = key_rows[:, None, :, None] * GRID_W + key_cols[None, :, None, :]
    k_blk = k_rot[:, :, tok]
    v_blk = v[:, :, tok]
    q_cols = j[:, None] * NA_QBLOCK_W + jnp.arange(NA_QBLOCK_W)[None, :]
    win_c0 = jnp.clip(q_cols - NA_WIN_W // 2, 0, GRID_W - NA_WIN_W)
    kc = key_cols[:, None, :]
    in_win = (kc >= win_c0[:, :, None]) & (kc < win_c0[:, :, None] + NA_WIN_W)
    dr_idx = key_rows - r[:, None] + NA_WIN_H - 1
    dc_idx = jnp.clip(kc - q_cols[:, :, None] + NA_WIN_W - 1, 0, 2 * NA_WIN_W - 2)
    bias = rpb[:, dr_idx[:, None, None, :, None], dc_idx[None, :, :, None, :]]
    q_blk = q_rot.reshape(bsz, nh, rows, ncb, NA_QBLOCK_W, dh)
    s_win = jnp.einsum('bhrjqd,bhrjakd->bhrjqak', q_blk, k_blk).astype(jnp.float32) * scale
    s_win = jnp.where(in_win[:, :, None, :], s_win + bias.astype(jnp.float32), -jnp.inf)
    q_plain = q.reshape(bsz, nh, rows, ncb, NA_QBLOCK_W, dh)
    s_ctx = jnp.einsum('bhrjqd,bhld->bhrjql', q_plain, k_ctx).astype(jnp.float32) * scale
    n_win = kh * NA_KSPAN_W
    s_all = jnp.concatenate([s_win.reshape(bsz, nh, rows, ncb, NA_QBLOCK_W, n_win), s_ctx], axis=-1)
    p = jax.nn.softmax(s_all, axis=-1).astype(v.dtype)
    p_win = p[..., :n_win].reshape(bsz, nh, rows, ncb, NA_QBLOCK_W, kh, NA_KSPAN_W)
    o = (jnp.einsum('bhrjqak,bhrjakd->bhrjqd', p_win, v_blk)
         + jnp.einsum('bhrjql,bhld->bhrjqd', p[..., n_win:], v_ctx))
    return from_heads(o.reshape(bsz, nh, seq, dh))

def context_attention(q, k, v):
    scale = q.shape[-1] ** -0.5
    s = jnp.einsum('bhld,bhmd->bhlm', q, k).astype(jnp.float32) * scale
    p = jax.nn.softmax(s, axis=-1).astype(v.dtype)
    return jnp.einsum('bhlm,bhmd->bhld', p, v)

def log_forget(z, lb):
    lb_h = lb.reshape(N_HG_HEADS, 1, HG_DK)
    return jnp.log(lb_h + (1.0 - lb_h) * jax.nn.sigmoid(z.astype(jnp.float32)))

def gla_chunked(q, k, v, log_f, s0):
    bsz, nh, seq, dk = q.shape
    dv = v.shape[-1]
    n = seq // HG_CHUNK
    qc = q.astype(jnp.float32).reshape(bsz, nh, n, HG_CHUNK, dk)
    kc = k.astype(jnp.float32).reshape(bsz, nh, n, HG_CHUNK, dk)
    vc = v.astype(jnp.float32).reshape(bsz, nh, n, HG_CHUNK, dv)
    b = jnp.cumsum(log_f.reshape(bsz, nh, n, HG_CHUNK, dk), axis=3)
    b_end = b[:, :, :, -1:, :]
    q_dec = qc * jnp.exp(b)
    k_dec = kc * jnp.exp(-b)
    idx = jnp.arange(HG_CHUNK)
    lower = idx[:, None] >= idx[None, :]
    a = jnp.where(lower, jnp.einsum('bhnck,bhnsk->bhncs', q_dec, k_dec), 0.0)
    o_intra = jnp.einsum('bhncs,bhnsv->bhncv', a, vc)
    kv = jnp.einsum('bhnck,bhncv->bhnkv', kc * jnp.exp(b_end - b), vc)
    decay = jnp.exp(b_end[:, :, :, 0, :])

    def step(s, inp):
        dec, upd = inp
        return dec[..., None] * s + upd, s

    s_fin, s_prev = lax.scan(step, s0.astype(jnp.float32),
                             (jnp.moveaxis(decay, 2, 0), jnp.moveaxis(kv, 2, 0)))
    s_prev = jnp.moveaxis(s_prev, 0, 2)
    o_inter = jnp.einsum('bhnck,bhnkv->bhncv', q_dec, s_prev)
    return (o_intra + o_inter).reshape(bsz, nh, seq, dv), s_fin

def hgrn2_bidir(q, z_fwd, z_bwd, i, lb, s0_fwd, s0_bwd):
    lf_f = log_forget(z_fwd, lb)
    lf_b = log_forget(z_bwd, lb)
    o_f, s_f = gla_chunked(q, -jnp.expm1(lf_f), i, lf_f, s0_fwd)
    flip = lambda t: jnp.flip(t, axis=2)
    o_b, s_b = gla_chunked(flip(q), flip(-jnp.expm1(lf_b)), flip(i), flip(lf_b), s0_bwd)
    return o_f + flip(o_b), s_f, s_b

def hgrn2_readout(o, g, norm_g):
    return from_heads(rms_norm(o.astype(g.dtype), norm_g) * jax.nn.sigmoid(g))

def ec_moe(h, w_router, w_gate, w_up, w_down):
    bsz, n_tok, d = h.shape
    cap = EC_CAPACITY_FACTOR * n_tok // N_EXPERTS
    aff = jax.nn.softmax(jnp.einsum('btd,de->bte', h, w_router).astype(jnp.float32), axis=-1)
    gate, idx = lax.top_k(jnp.swapaxes(aff, 1, 2), cap)
    xs = jax.vmap(lambda hb, ib: hb[ib])(h, idx)
    hid = (jax.nn.silu(jnp.einsum('becd,edf->becf', xs, w_gate))
           * jnp.einsum('becd,edf->becf', xs, w_up))
    y = jnp.einsum('becf,efd->becd', hid, w_down) * gate[..., None].astype(h.dtype)
    return jax.vmap(lambda yb, ib: jnp.zeros((n_tok, d), y.dtype).at[ib.reshape(-1)].add(yb.reshape(-1, d)))(y, idx)

def first_inputs(seed: int = 0) -> dict:
    key = jax.random.key(seed)
    ks = jax.random.split(key, 19)
    nrm = jax.random.normal
    d = D_MODEL
    f32 = jnp.float32
    return {
        'x': nrm(ks[0], (BATCH, SEQ, d), f32),
        'c': nrm(ks[1], (BATCH, d), f32),
        'ctx': nrm(ks[2], (BATCH, CTX_LEN, d), f32),
        'c_ctx': nrm(ks[3], (d,), f32),
        'w_mod': 0.5 * d ** -0.5 * nrm(ks[4], (DEPTH, d, 6 * d), f32),
        'b_mod': 0.01 * nrm(ks[5], (DEPTH, 6 * d), f32),
        'g_pre1': 1.0 + 0.05 * nrm(ks[6], (DEPTH, d), f32),
        'g_post1': 1.0 + 0.05 * nrm(ks[7], (DEPTH, d), f32),
        'g_pre2': 1.0 + 0.05 * nrm(ks[8], (DEPTH, d), f32),
        'g_post2': 1.0 + 0.05 * nrm(ks[9], (DEPTH, d), f32),
        'w_in': d ** -0.5 * nrm(ks[10], (DEPTH, d, IN_COLS), f32),
        'w_out': MIX_WIDTH ** -0.5 * nrm(ks[11], (DEPTH, MIX_WIDTH, d), f32),
        'na_rpb': 0.1 * nrm(ks[12], (DEPTH, N_NA_HEADS, 2 * NA_WIN_H - 1, 2 * NA_WIN_W - 1), f32),
        'hg_lb_logits': 0.5 * nrm(ks[13], (DEPTH + 1, HG_KEY_WIDTH), f32),
        'hg_norm': 1.0 + 0.05 * nrm(ks[14], (DEPTH, HG_DV), f32),
        'w_router': d ** -0.5 * nrm(ks[15], (DEPTH, d, N_EXPERTS), f32),
        'w_gate': d ** -0.5 * nrm(ks[16], (DEPTH, N_EXPERTS, d, D_EXPERT), f32),
        'w_up': d ** -0.5 * nrm(ks[17], (DEPTH, N_EXPERTS, d, D_EXPERT), f32),
        'w_down': D_EXPERT ** -0.5 * nrm(ks[18], (DEPTH, N_EXPERTS, D_EXPERT, d), f32),
    }

def first_block(x, c, ctx, c_ctx, w_mod, b_mod, g_pre1, g_post1, g_pre2, g_post2, w_in, w_out,
              na_rpb, hg_lb_logits, hg_norm, w_router, w_gate, w_up, w_down):
    bsz = x.shape[0]
    silu_c = jax.nn.silu(c)
    silu_cc = jax.nn.silu(c_ctx)
    lb_all = jnp.cumsum(jax.nn.softmax(hg_lb_logits.astype(jnp.float32), axis=0), axis=0)
    for l in range(DEPTH):
        mod = silu_c @ w_mod[l] + b_mod[l]
        mod_c = silu_cc @ w_mod[l] + b_mod[l]
        sh1, sc1, gt1, sh2, sc2, gt2 = jnp.split(mod[:, None, :], 6, axis=-1)
        sh1c, sc1c, gt1c, sh2c, sc2c, gt2c = jnp.split(mod_c, 6)
        lb = lb_all[l]

        h = modulate(rms_norm(x, g_pre1[l]), sh1, sc1)
        hc = modulate(rms_norm(ctx, g_pre1[l]), sh1c, sc1c)
        qn, kn, vn, qh, zf, zb, ih, gh = split_cols(h @ w_in[l])
        qn_c, kn_c, vn_c, qh_c, zf_c, zb_c, ih_c, gh_c = split_cols(hc @ w_in[l])
        kn_ch = to_heads(kn_c, N_NA_HEADS)
        vn_ch = to_heads(vn_c, N_NA_HEADS)

        na_o = neighbourhood_attention(to_heads(qn, N_NA_HEADS), to_heads(kn, N_NA_HEADS),
                                       to_heads(vn, N_NA_HEADS), kn_ch, vn_ch, na_rpb[l])

        s0 = jnp.zeros((bsz, N_HG_HEADS, HG_DK, HG_DV), jnp.float32)
        o_hc, s_cf, s_cb = hgrn2_bidir(to_heads(qh_c, N_HG_HEADS), to_heads(zf_c, N_HG_HEADS),
                                       to_heads(zb_c, N_HG_HEADS), to_heads(ih_c, N_HG_HEADS), lb, s0, s0)
        o_hl, _, _ = hgrn2_bidir(to_heads(qh, N_HG_HEADS), to_heads(zf, N_HG_HEADS),
                                 to_heads(zb, N_HG_HEADS), to_heads(ih, N_HG_HEADS), lb, s_cf, s_cb)
        hg_o = hgrn2_readout(o_hl, to_heads(gh, N_HG_HEADS), hg_norm[l])

        mix = jnp.concatenate([na_o, hg_o], axis=-1) @ w_out[l]
        x = x + gt1 * rms_norm(mix, g_post1[l])

        h2 = modulate(rms_norm(x, g_pre2[l]), sh2, sc2)
        x = x + gt2 * rms_norm(ec_moe(h2, w_router[l], w_gate[l], w_up[l], w_down[l]), g_post2[l])

        if l < DEPTH - 1:
            o_cna = context_attention(to_heads(qn_c, N_NA_HEADS), kn_ch, vn_ch)
            hg_oc = hgrn2_readout(o_hc, to_heads(gh_c, N_HG_HEADS), hg_norm[l])
            mix_c = jnp.concatenate([from_heads(o_cna), hg_oc], axis=-1) @ w_out[l]
            ctx = ctx + gt1c * rms_norm(mix_c, g_post1[l])
            hc2 = modulate(rms_norm(ctx, g_pre2[l]), sh2c, sc2c)
            ctx = ctx + gt2c * rms_norm(ec_moe(hc2, w_router[l], w_gate[l], w_up[l], w_down[l]), g_post2[l])
    return x


DEPTH_2 = 2

EPS = 1e-6

A_HEADS = 4
A_HEAD_DIM = 128
A_WIDTH = A_HEADS * A_HEAD_DIM
SHORT_CONV_W = 5
DELTA_CHUNK = 64
B_Q_HEADS = 8
B_KV_HEADS = 2
B_HEAD_DIM = 64
B_GROUP = B_Q_HEADS // B_KV_HEADS
B_WIDTH = B_Q_HEADS * B_HEAD_DIM
B_KV_WIDTH = B_KV_HEADS * B_HEAD_DIM
ROPE_AXIS_PAIRS = B_HEAD_DIM // 4
ROPE_THETA = 10000.0
Q_BLOCK = 128
OFF_Z_A = 3 * A_WIDTH
OFF_BA_A = OFF_Z_A + A_WIDTH
OFF_Q_B = OFF_BA_A + 4 * A_HEADS
OFF_K_B = OFF_Q_B + B_WIDTH
OFF_V_B = OFF_K_B + B_KV_WIDTH
HYB_IN_WIDTH = OFF_V_B + B_KV_WIDTH
MIX_WIDTH_2 = A_WIDTH + B_WIDTH
CONF_WIDTH = D_MODEL
CONF_KERNEL = 31
FFN_HIDDEN = ((8 * D_MODEL + 3 * 256 - 1) // (3 * 256)) * 256
N_EVEN = (DEPTH_2 + 1) // 2
N_ODD = DEPTH_2 // 2


F32 = jnp.float32

def rms_norm_2(x, gain):
    xf = x.astype(F32)
    y = xf * lax.rsqrt(jnp.mean(jnp.square(xf), axis=-1, keepdims=True) + EPS)
    return (y * gain.astype(F32)).astype(x.dtype)

def layer_norm(x, gain, bias):
    xf = x.astype(F32)
    mu = jnp.mean(xf, axis=-1, keepdims=True)
    var = jnp.mean(jnp.square(xf - mu), axis=-1, keepdims=True)
    return ((xf - mu) * lax.rsqrt(var + EPS) * gain.astype(F32) + bias.astype(F32)).astype(x.dtype)

def l2_normalize(x):
    return x * lax.rsqrt(jnp.sum(jnp.square(x), axis=-1, keepdims=True) + EPS)

def depthwise_conv_centred(x, w):
    pad = w.shape[0] // 2
    return lax.conv_general_dilated(
        x, w[:, None, :].astype(x.dtype), window_strides=(1,), padding=[(pad, pad)],
        dimension_numbers=("NWC", "WIO", "NWC"), feature_group_count=x.shape[-1])

def ada_terms(cond, w_mod, b_mod):
    m = jax.nn.silu(cond) @ w_mod + b_mod
    return jnp.split(m, 6, axis=-1)

def modulate_2(h, shift, scale):
    return h * (1.0 + scale) + shift

def axial_rope_tables(n_tokens):
    rows = n_tokens // GRID_W
    row = jnp.broadcast_to(jnp.arange(rows, dtype=F32)[:, None], (rows, GRID_W)).reshape(n_tokens)
    col = jnp.broadcast_to(jnp.arange(GRID_W, dtype=F32)[None, :], (rows, GRID_W)).reshape(n_tokens)
    inv_freq = ROPE_THETA ** (-jnp.arange(ROPE_AXIS_PAIRS, dtype=F32) / ROPE_AXIS_PAIRS)
    ang_r = row[:, None] * inv_freq
    ang_c = col[:, None] * inv_freq
    ang = jnp.concatenate([ang_r, ang_r, ang_c, ang_c], axis=-1)
    return jnp.cos(ang), jnp.sin(ang)

def apply_axial_rope(x, cos, sin):
    xf = x.astype(F32)
    xr = xf.reshape(*x.shape[:-1], 2, 2, ROPE_AXIS_PAIRS)
    rot = jnp.stack([-xr[..., 1, :], xr[..., 0, :]], axis=-2).reshape(x.shape)
    return (xf * cos[None, :, None, :] + rot * sin[None, :, None, :]).astype(x.dtype)

def gated_delta_chunked(q, k, v, g, beta, s0, need_out):
    bsz, n_tok, n_h, _ = q.shape
    dv = v.shape[-1]
    n_ch = n_tok // DELTA_CHUNK

    def chunks(t):
        return t.reshape(bsz, n_ch, DELTA_CHUNK, n_h, -1).transpose(1, 0, 3, 2, 4)

    qc, kc, vc = chunks(q), chunks(k), chunks(v)
    gcum = jnp.cumsum(chunks(g[..., None])[..., 0], axis=-1)
    bc = chunks(beta[..., None])
    idx = jnp.arange(DELTA_CHUNK)
    incl = idx[:, None] >= idx[None, :]
    strict = idx[:, None] > idx[None, :]
    decay = jnp.exp(jnp.where(incl, gcum[..., :, None] - gcum[..., None, :], -jnp.inf))
    kb = kc * bc
    lower = jnp.where(strict, jnp.einsum("nbhcd,nbhsd->nbhcs", kb, kc) * decay, 0.0)
    eye = jnp.eye(DELTA_CHUNK, dtype=F32)
    rhs = jnp.concatenate([vc * bc, kb * jnp.exp(gcum)[..., None]], axis=-1)
    sol = lax.linalg.triangular_solve(lower + eye, rhs, left_side=True, lower=True, unit_diagonal=True)
    u, w = sol[..., :dv], sol[..., dv:]
    g_last = gcum[..., -1]
    k_tail = kc * jnp.exp(g_last[..., None] - gcum)[..., None]
    xs = (u, w, k_tail, g_last)
    if need_out:
        intra = jnp.einsum("nbhcd,nbhsd->nbhcs", qc, kc) * decay
        q_dec = qc * jnp.exp(gcum)[..., None]
        xs = xs + (q_dec, intra)

    def step(state, xs_i):
        u_i, w_i, kt_i, gl_i = xs_i[:4]
        v_new = u_i - jnp.einsum("bhcd,bhde->bhce", w_i, state)
        new_state = state * jnp.exp(gl_i)[..., None, None] + jnp.einsum("bhcd,bhce->bhde", kt_i, v_new)
        if need_out:
            qd_i, a_i = xs_i[4:]
            o_i = jnp.einsum("bhcd,bhde->bhce", qd_i, state) + jnp.einsum("bhcs,bhse->bhce", a_i, v_new)
            return new_state, o_i
        return new_state, None

    s_fin, o = lax.scan(step, s0, xs)
    if need_out:
        o = o.transpose(1, 0, 3, 2, 4).reshape(bsz, n_tok, n_h, dv)
    return o, s_fin

def bidirectional_delta(q, k, v, g, beta, s0_fwd, s0_bwd, need_out):
    o_f, s_f = gated_delta_chunked(q, k, v, g[:, :, 0], beta[:, :, 0], s0_fwd, need_out)
    rev = lambda t: jnp.flip(t, axis=1)
    o_b, s_b = gated_delta_chunked(rev(q), rev(k), rev(v), rev(g[:, :, 1]), rev(beta[:, :, 1]), s0_bwd, need_out)
    o = o_f + rev(o_b) if need_out else None
    return o, s_f, s_b

def split_hybrid_projection(p, conv_w, a_log, dt_bias, q_norm, k_norm):
    bsz, n_tok, _ = p.shape
    qkv = jax.nn.silu(depthwise_conv_centred(p[..., :OFF_Z_A], conv_w))
    qkv = qkv.astype(F32).reshape(bsz, n_tok, 3, A_HEADS, A_HEAD_DIM)
    qa = l2_normalize(qkv[:, :, 0]) * (A_HEAD_DIM ** -0.5)
    ka = l2_normalize(qkv[:, :, 1])
    va = qkv[:, :, 2]
    za = p[..., OFF_Z_A:OFF_BA_A].reshape(bsz, n_tok, A_HEADS, A_HEAD_DIM)
    ba = p[..., OFF_BA_A:OFF_Q_B].astype(F32).reshape(bsz, n_tok, 2, 2, A_HEADS)
    beta = jax.nn.sigmoid(ba[:, :, 0])
    g = -jnp.exp(a_log.astype(F32)) * jax.nn.softplus(ba[:, :, 1] + dt_bias.astype(F32))
    qb = rms_norm_2(p[..., OFF_Q_B:OFF_K_B].reshape(bsz, n_tok, B_Q_HEADS, B_HEAD_DIM), q_norm)
    kb = rms_norm_2(p[..., OFF_K_B:OFF_V_B].reshape(bsz, n_tok, B_KV_HEADS, B_HEAD_DIM), k_norm)
    vb = p[..., OFF_V_B:].reshape(bsz, n_tok, B_KV_HEADS, B_HEAD_DIM)
    return qa, ka, va, za, g, beta, qb, kb, vb

def attend(q, k, v):
    s = jnp.einsum("bqkgd,bskd->bkgqs", q, k, preferred_element_type=F32) * (B_HEAD_DIM ** -0.5)
    p = jax.nn.softmax(s, axis=-1).astype(v.dtype)
    return jnp.einsum("bkgqs,bskd->bqkgd", p, v)

def latent_attention_blocks(q, k, v):
    bsz, n_tok = q.shape[:2]
    nb = n_tok // Q_BLOCK
    qb = q.reshape(bsz, nb, Q_BLOCK, *q.shape[2:]).swapaxes(0, 1)
    o = lax.map(lambda blk: attend(blk, k, v), qb)
    return o.swapaxes(0, 1).reshape(bsz, n_tok, B_WIDTH)

def hybrid_mixer(a_lat, a_ctx, w_in, conv_w, a_log, dt_bias, out_norm, q_norm, k_norm, w_out, cos, sin, ctx_out):
    bsz, n_tok, _ = a_lat.shape
    n_ctx = a_ctx.shape[1]
    qa_l, ka_l, va_l, za_l, g_l, be_l, qb_l, kb_l, vb_l = split_hybrid_projection(
        a_lat @ w_in, conv_w, a_log, dt_bias, q_norm, k_norm)
    qa_c, ka_c, va_c, za_c, g_c, be_c, qb_c, kb_c, vb_c = split_hybrid_projection(
        a_ctx @ w_in, conv_w, a_log, dt_bias, q_norm, k_norm)

    zeros = jnp.zeros((bsz, A_HEADS, A_HEAD_DIM, A_HEAD_DIM), F32)
    o_ctx_a, s_fwd, s_bwd = bidirectional_delta(qa_c, ka_c, va_c, g_c, be_c, zeros, zeros, ctx_out)
    o_lat_a, _, _ = bidirectional_delta(qa_l, ka_l, va_l, g_l, be_l, s_fwd, s_bwd, True)

    def delta_readout(o, z, n):
        y = rms_norm_2(o, out_norm) * jax.nn.silu(z.astype(F32))
        return y.reshape(bsz, n, A_WIDTH).astype(a_lat.dtype)

    qb_l = apply_axial_rope(qb_l, cos, sin)
    kb_l = apply_axial_rope(kb_l, cos, sin)
    k_all = jnp.concatenate([kb_c, kb_l], axis=1)
    v_all = jnp.concatenate([vb_c, vb_l], axis=1)
    group = lambda t: t.reshape(*t.shape[:2], B_KV_HEADS, B_GROUP, B_HEAD_DIM)
    o_lat_b = latent_attention_blocks(group(qb_l), k_all, v_all)

    y_lat = jnp.concatenate([delta_readout(o_lat_a, za_l, n_tok), o_lat_b.astype(a_lat.dtype)], axis=-1) @ w_out
    y_ctx = None
    if ctx_out:
        o_ctx_b = attend(group(qb_c), kb_c, vb_c).reshape(bsz, n_ctx, B_WIDTH)
        y_ctx = jnp.concatenate([delta_readout(o_ctx_a, za_c, n_ctx), o_ctx_b.astype(a_ctx.dtype)], axis=-1) @ w_out
    return y_lat, y_ctx

def conformer_conv(h, w_in, b_in, dw_w, dw_b, ln_g, ln_b, w_out, b_out):
    val, gate = jnp.split(h @ w_in + b_in, 2, axis=-1)
    u = val * jax.nn.sigmoid(gate)
    u = depthwise_conv_centred(u, dw_w) + dw_b
    u = jax.nn.silu(layer_norm(u, ln_g, ln_b))
    return u @ w_out + b_out

def swiglu_ffn(h, w_in, w_out):
    gate, up = jnp.split(h @ w_in, 2, axis=-1)
    return (jax.nn.silu(gate) * up) @ w_out

def second_inputs(seed: int = 0) -> dict:
    key = jax.random.key(seed)
    ks = iter(jax.random.split(key, 40))
    D = D_MODEL

    def nrm(shape, scale):
        return jax.random.normal(next(ks), shape, F32) * scale

    def gain(shape):
        return 1.0 + nrm(shape, 0.05)

    a_log = jnp.log(jax.random.uniform(next(ks), (N_EVEN, 2, A_HEADS), F32, 1.0, 16.0))
    dt = jnp.exp(jax.random.uniform(next(ks), (N_EVEN, 2, A_HEADS), F32, math.log(1e-3), math.log(1e-1)))
    dt_bias = dt + jnp.log(-jnp.expm1(-dt))
    return {
        "x": nrm((BATCH, SEQ, D), 1.0),
        "c": nrm((BATCH, D), 1.0),
        "ctx": nrm((BATCH, CTX_LEN, D), 1.0),
        "c_ctx": nrm((D,), 1.0),
        "w_mod": nrm((DEPTH_2, D, 6 * D), 0.5 * D ** -0.5),
        "b_mod": nrm((DEPTH_2, 6 * D), 0.02),
        "g_mix_pre": gain((DEPTH_2, D)),
        "g_mix_post": gain((DEPTH_2, D)),
        "g_ffn_pre": gain((DEPTH_2, D)),
        "g_ffn_post": gain((DEPTH_2, D)),
        "w_ffn_in": nrm((DEPTH_2, D, 2 * FFN_HIDDEN), D ** -0.5),
        "w_ffn_out": nrm((DEPTH_2, FFN_HIDDEN, D), FFN_HIDDEN ** -0.5),
        "hyb_w_in": nrm((N_EVEN, D, HYB_IN_WIDTH), D ** -0.5),
        "hyb_conv_w": nrm((N_EVEN, SHORT_CONV_W, 3 * A_WIDTH), SHORT_CONV_W ** -0.5),
        "hyb_a_log": a_log,
        "hyb_dt_bias": dt_bias,
        "hyb_out_norm": gain((N_EVEN, A_HEAD_DIM)),
        "hyb_q_norm": gain((N_EVEN, B_HEAD_DIM)),
        "hyb_k_norm": gain((N_EVEN, B_HEAD_DIM)),
        "hyb_w_out": nrm((N_EVEN, MIX_WIDTH_2, D), MIX_WIDTH_2 ** -0.5),
        "conf_w_in": nrm((N_ODD, D, 2 * CONF_WIDTH), D ** -0.5),
        "conf_b_in": nrm((N_ODD, 2 * CONF_WIDTH), 0.02),
        "conf_dw_w": nrm((N_ODD, CONF_KERNEL, CONF_WIDTH), CONF_KERNEL ** -0.5),
        "conf_dw_b": nrm((N_ODD, CONF_WIDTH), 0.02),
        "conf_ln_g": gain((N_ODD, CONF_WIDTH)),
        "conf_ln_b": nrm((N_ODD, CONF_WIDTH), 0.02),
        "conf_w_out": nrm((N_ODD, CONF_WIDTH, D), CONF_WIDTH ** -0.5),
        "conf_b_out": nrm((N_ODD, D), 0.02),
    }

def second_block(x, c, ctx, c_ctx, w_mod, b_mod, g_mix_pre, g_mix_post, g_ffn_pre, g_ffn_post, w_ffn_in, w_ffn_out,
              hyb_w_in, hyb_conv_w, hyb_a_log, hyb_dt_bias, hyb_out_norm, hyb_q_norm, hyb_k_norm, hyb_w_out,
              conf_w_in, conf_b_in, conf_dw_w, conf_dw_b, conf_ln_g, conf_ln_b, conf_w_out, conf_b_out):
    cos, sin = axial_rope_tables(x.shape[1])
    h, hc = x, ctx
    for layer in range(DEPTH_2):
        is_hybrid = layer % 2 == 0
        idx = layer // 2
        advance_ctx = any(j % 2 == 0 for j in range(layer + 1, DEPTH_2))
        sh1, sc1, gt1, sh2, sc2, gt2 = ada_terms(c[:, None, :], w_mod[layer], b_mod[layer])
        a = modulate_2(rms_norm_2(h, g_mix_pre[layer]), sh1, sc1)
        if is_hybrid or advance_ctx:
            csh1, csc1, cgt1, csh2, csc2, cgt2 = ada_terms(c_ctx, w_mod[layer], b_mod[layer])
            ac = modulate_2(rms_norm_2(hc, g_mix_pre[layer]), csh1, csc1)
        if is_hybrid:
            y, yc = hybrid_mixer(a, ac, hyb_w_in[idx], hyb_conv_w[idx], hyb_a_log[idx], hyb_dt_bias[idx],
                                 hyb_out_norm[idx], hyb_q_norm[idx], hyb_k_norm[idx], hyb_w_out[idx],
                                 cos, sin, advance_ctx)
        else:
            conf = (conf_w_in[idx], conf_b_in[idx], conf_dw_w[idx], conf_dw_b[idx],
                    conf_ln_g[idx], conf_ln_b[idx], conf_w_out[idx], conf_b_out[idx])
            y = conformer_conv(a, *conf)
            yc = conformer_conv(ac, *conf) if advance_ctx else None
        h = h + gt1 * rms_norm_2(y, g_mix_post[layer])
        f = swiglu_ffn(modulate_2(rms_norm_2(h, g_ffn_pre[layer]), sh2, sc2), w_ffn_in[layer], w_ffn_out[layer])
        h = h + gt2 * rms_norm_2(f, g_ffn_post[layer])
        if advance_ctx:
            hc = hc + cgt1 * rms_norm_2(yc, g_mix_post[layer])
            fc = swiglu_ffn(modulate_2(rms_norm_2(hc, g_ffn_pre[layer]), csh2, csc2), w_ffn_in[layer], w_ffn_out[layer])
            hc = hc + cgt2 * rms_norm_2(fc, g_ffn_post[layer])
    return h


def setup_inputs(seed=0):
    out = dict(first_inputs(seed))
    for name, value in second_inputs(seed + 1).items():
        if name != "x":
            out[name + "_2"] = value
    return out


def reference(
    x, c, ctx, c_ctx, w_mod, b_mod, g_pre1, g_post1, g_pre2, g_post2, w_in, w_out, na_rpb,
    hg_lb_logits, hg_norm, w_router, w_gate, w_up, w_down, c_2, ctx_2, c_ctx_2, w_mod_2,
    b_mod_2, g_mix_pre_2, g_mix_post_2, g_ffn_pre_2, g_ffn_post_2, w_ffn_in_2, w_ffn_out_2,
    hyb_w_in_2, hyb_conv_w_2, hyb_a_log_2, hyb_dt_bias_2, hyb_out_norm_2, hyb_q_norm_2,
    hyb_k_norm_2, hyb_w_out_2, conf_w_in_2, conf_b_in_2, conf_dw_w_2, conf_dw_b_2, conf_ln_g_2,
    conf_ln_b_2, conf_w_out_2, conf_b_out_2,
):
    x = first_block(
        x, c, ctx, c_ctx, w_mod, b_mod, g_pre1, g_post1, g_pre2, g_post2, w_in, w_out, na_rpb,
        hg_lb_logits, hg_norm, w_router, w_gate, w_up, w_down,
    )
    return second_block(
        x, c_2, ctx_2, c_ctx_2, w_mod_2, b_mod_2, g_mix_pre_2, g_mix_post_2, g_ffn_pre_2,
        g_ffn_post_2, w_ffn_in_2, w_ffn_out_2, hyb_w_in_2, hyb_conv_w_2, hyb_a_log_2,
        hyb_dt_bias_2, hyb_out_norm_2, hyb_q_norm_2, hyb_k_norm_2, hyb_w_out_2, conf_w_in_2,
        conf_b_in_2, conf_dw_w_2, conf_dw_b_2, conf_ln_g_2, conf_ln_b_2, conf_w_out_2,
        conf_b_out_2,
    )


_drawn_inputs = setup_inputs


def setup_inputs(seed=0):
    import zlib

    import numpy as np

    out = dict(_drawn_inputs(seed))
    spreads = {}
    factors = {'g_post2': 3.549,
     'na_rpb': 2.743,
     'g_mix_post_2': 3.069,
     'g_ffn_post_2': 3.176,
     'hyb_out_norm_2': 3.691,
     'hyb_q_norm_2': 8.0,
     'hyb_k_norm_2': 8.0,
     'conf_b_in_2': 8.0,
     'conf_dw_b_2': 6.138,
     'conf_ln_g_2': 3.679,
     'conf_ln_b_2': 22.199,
     'conf_b_out_2': 6.683}
    for name, (base, spread) in spreads.items():
        noise = np.random.default_rng([zlib.crc32(name.encode()), seed]).standard_normal(out[name].shape)
        drawn = base * np.exp(spread * noise) if base else spread * noise
        out[name] = jnp.asarray(drawn.astype(out[name].dtype))
    for name, factor in factors.items():
        out[name] = (out[name] * factor).astype(out[name].dtype)
    return out
```

```python
import numpy as np
import concourse.bass as bass
from concourse import mybir
from contextlib import ExitStack


F32 = mybir.dt.float32
U32 = mybir.dt.uint32
ALU = mybir.AluOpType
ACT = mybir.ActivationFunctionType
AX = mybir.AxisListType

P = 128
D = 1024
KT = D // P
SEQ = 256
TT = SEQ // P
HALF = 512
NA_HEADS, HEAD = 8, 64
HG_HEADS, HG_CHUNK = 4, 32
N_EXPERTS, CAP, D_EXPERT = 16, 32, 2752
COLG = D_EXPERT // 4
GCH = COLG // 2
QMAIN = COLG // P
TAIL = COLG - QMAIN * P
FFN = 2816
FT = FFN // P
MOD_COLS = 6 * D
MODQ = MOD_COLS // 4
CONF_K = 31
SHORT_K = 5
PADW = SEQ + SHORT_K - 1
UPAD = SEQ + CONF_K - 1
EPS = 1e-6
DELTA_CHUNK = 64
N_LEVELS = 6

SLOT = 3072
RING = 6
ROTATING = 6



def constants():
    t = np.arange(P)
    a, b = t[:, None], t[None, :]
    c32, c64 = (a // 32 == b // 32), (a // 64 == b // 64)
    parts = {
        "ident": a == b,
        "ones": a * 0 + b * 0 + 1,
        "first": (a % 32 == 0) & (b >= 0),
        "after": a > b, "before": a < b,
        "pre32_0": (a <= b) & c32, "pre32_1": (a >= b) & c32,
        "suf32_0": (a > b) & c32, "suf32_1": (a < b) & c32,
        "pre64_0": (a <= b) & c64, "pre64_1": (a >= b) & c64,
        "suf64_0": (a > b) & c64, "suf64_1": (a < b) & c64,
        "chunk32": a // 32 == np.arange(4)[None, :],
        "iota": np.broadcast_to(np.arange(CAP)[None, :], (P, CAP)),
        "slot": a % CAP,
    }
    for k in range(N_LEVELS):
        w = 1 << k
        m = (a // (2 * w) == b // (2 * w)) & (a // w % 2 == 1) & (b // w % 2 == 0)
        parts[f"level{k}_0"] = m
        parts[f"level{k}_1"] = m.T
    tok = np.arange(SEQ)
    freq = (10000.0 ** (-np.arange(16, dtype=np.float32) / 16)).astype(np.float32)
    rows = (tok // 64).astype(np.float32)[:, None] * freq
    cols = (tok % 64).astype(np.float32)[:, None] * freq
    cos = np.concatenate([np.cos(rows)] * 2 + [np.cos(cols)] * 2, 1)
    sin = np.concatenate([-np.sin(rows), np.sin(rows), -np.sin(cols), np.sin(cols)], 1)
    for i in range(TT):
        parts[f"cos{i}"] = cos[i * P:(i + 1) * P]
        parts[f"sin{i}"] = sin[i * P:(i + 1) * P]
    qc = (t % 64)[:, None]
    kc = np.arange(64)[None, :]
    w0 = np.clip(qc - 8, 0, 48)
    parts["window"] = np.where((kc >= w0) & (kc < w0 + 16), 0.0, -1e30)
    at, places = 0, {}
    for name, v in parts.items():
        places[name] = (at, v.shape[1])
        at += v.shape[1]
    return np.ascontiguousarray(np.concatenate([v.astype(np.float32) for v in parts.values()], 1)), places


CONSTS, CONST_AT = constants()

COLS = [("c1", KT * 32), ("c2", KT * 32), ("g_pre1", KT), ("g_pre2", KT), ("g_mix0", KT), ("g_mix1", KT),
        ("g_ffn0", KT), ("g_ffn1", KT), ("conf_b_in", 2 * KT), ("conf_dw_b", KT), ("ln_g", KT), ("ln_b", KT),
        ("conf_dw_w", KT * CONF_K), ("conv_w", 12 * SHORT_K), ("w_router", KT * N_EXPERTS)]
ROWS = [("hg_norm", 128), ("logit0", 512), ("logit1", 512), ("out_norm", 128), ("q_norm", 64), ("k_norm", 64),
        ("a_log", 8), ("dt_bias", 8)]


def places_of(parts):
    at, places = 0, {}
    for name, n in parts:
        places[name] = (at, n)
        at += n
    return places, at


COL_AT, N_COLS = places_of(COLS)
ROW_AT, N_ROWS = places_of(ROWS)


def program(nc, T, out):
    ctx = ExitStack()
    with ctx:
        def sb(name, n):
            return ctx.enter_context(nc.sbuf_tensor(name, [P, n], F32))

        def semaphore(name):
            return ctx.enter_context(nc.semaphore(name))

        ring = sb("ring", RING * SLOT)
        consts = sb("consts", CONSTS.shape[1])
        cols = sb("cols", N_COLS)
        rows = sb("rows", N_ROWS)
        x = sb("x", TT * D)
        gates = sb("gates", 2 * D)
        modcol = sb("modcol", 96)
        shsc = sb("shsc", 32)
        small = sb("small", 760)
        A = sb("arena", 23552)
        psum = ctx.enter_context(nc.psum_tensor("psum", [P, 8, HALF], F32))

        bank_filled = [semaphore(f"bank{b}_filled") for b in range(8)]
        bank_drained = [semaphore(f"bank{b}_drained") for b in range(8)]
        slot_loaded = [semaphore(f"slot{s}_loaded") for s in range(RING)]
        weights_used = semaphore("weights_used")
        vector_done = semaphore("vector_done")
        scalar_done = semaphore("scalar_done")
        pool_done = semaphore("pool_done")
        consts_loaded = semaphore("consts_loaded")
        normed_ready = semaphore("normed_ready")
        normed_second_ready = semaphore("normed_second_ready")
        mix_ready = semaphore("mix_ready")
        mod_rows_ready = semaphore("mod_rows_ready")
        cond_ready = semaphore("cond_ready")
        rotated = semaphore("rotated")
        log_forget_ready = semaphore("log_forget_ready")
        key_decayed = semaphore("key_decayed")
        query_key_decayed = semaphore("query_key_decayed")
        hgrn_state_read = semaphore("hgrn_state_read")
        affinity_ready = semaphore("affinity_ready")
        position_ready = semaphore("position_ready")
        selection_ready = semaphore("selection_ready")
        short_conv_ready = semaphore("short_conv_ready")
        grouped_query_ready = semaphore("grouped_query_ready")
        grouped_key_ready = semaphore("grouped_key_ready")
        log_decay_ready = semaphore("log_decay_ready")
        unit_qk_ready = semaphore("unit_qk_ready")
        decay_rows_ready = semaphore("decay_rows_ready")
        decay_cols_ready = semaphore("decay_cols_ready")
        query_decayed = semaphore("query_decayed")
        coupling_ready = semaphore("coupling_ready")
        kv_scaled = semaphore("kv_scaled")
        delta_state_ready = semaphore("delta_state_ready")
        delta_out_added = semaphore("delta_out_added")
        diag_ready = semaphore("diag_ready")
        diag_used = semaphore("diag_used")
        conv_out_ready = semaphore("conv_out_ready")
        mod_bias_loaded = semaphore("mod_bias_loaded")
        mod_cols_ready = semaphore("mod_cols_ready")
        post_gains_loaded = semaphore("post_gains_loaded")
        mean_square_ready = semaphore("mean_square_ready")
        root_ready = semaphore("root_ready")
        square_sum_ready = semaphore("square_sum_ready")
        rms_ready = semaphore("rms_ready")
        x_ready = semaphore("x_ready")
        row_max = semaphore("row_max")
        mod_bias_zeroed = semaphore("mod_bias_zeroed")
        cols_loaded = semaphore("cols_loaded")
        rows_loaded = semaphore("rows_loaded")
        x_loaded = semaphore("x_loaded")
        ctx_loaded = semaphore("ctx_loaded")
        bias_ready = semaphore("bias_ready")
        bound_in = semaphore("bound_in")
        bound_ready = semaphore("bound_ready")
        sigmoid_ready = semaphore("sigmoid_ready")
        forget_ready = semaphore("forget_ready")
        intra_zeroed = semaphore("intra_zeroed")
        squares_ready = semaphore("squares_ready")
        hgrn_gate = semaphore("hgrn_gate")
        affinity_exp = semaphore("affinity_exp")
        pads_zeroed = semaphore("pads_zeroed")
        short_conv_sum = semaphore("short_conv_sum")
        softplus_in = semaphore("softplus_in")
        softplus_exp = semaphore("softplus_exp")
        softplus_one = semaphore("softplus_one")
        softplus_log = semaphore("softplus_log")
        delta_gate = semaphore("delta_gate")
        conf_mean_in = semaphore("conf_mean_in")
        centred_ready = semaphore("centred_ready")
        layer_norm_ready = semaphore("layer_norm_ready")
        out_bias_loaded = semaphore("out_bias_loaded")
        out_ready = semaphore("out_ready")
        input_gate_ready = semaphore("input_gate_ready")
        conf_var_in = semaphore("conf_var_in")
        bias_loaded = semaphore("bias_loaded")
        stored = semaphore("stored")
        pv_done = {kind: semaphore(f"pv_done_{kind}") for kind in ("na", "gq")}

        def const(name):
            at, n = CONST_AT[name]
            return consts[:, at:at + n]

        def col(name):
            at, n = COL_AT[name]
            return cols[:, at:at + n]

        def row(name):
            at, n = ROW_AT[name]
            return rows[:, at:at + n]

        def R(at, n):
            return A[:, at:at + n]

        X = x[:, :].rearrange("p (t n) -> p t n", t=TT)
        G = gates[:, :].rearrange("p (g n) -> p g n", g=2)

        order, count_of, due = {}, {}, [0] * RING
        freed_by = {}

        def enlist(key):
            n = len(order)
            parts = 2 if key[0] in ("down", "ffn0", "ffn1", "conf") or key == ("hyb", "bkv") else 1
            order[key] = n
            due[n % RING] += 16 * parts
            count_of[key] = due[n % RING]

        def slot_of(key):
            return order[key] % RING

        def slot(i):
            return ring[:, i * SLOT:(i + 1) * SLOT]

        place = {}

        def bank_of(tag):
            return place[tag][0]

        def nth(tag):
            return place[tag][1] + 1

        def result(tag):
            return psum[:, bank_of(tag), :]

        class Tally:

            def __init__(self):
                self.given, self.had = {}, {}

            def gave(self, signal):
                self.given[signal] = self.given.get(signal, 0) + 1
                return self.given[signal]

            def due(self, signal, times=1):
                self.had[signal] = self.had.get(signal, 0) + times
                return self.had[signal]

        block = ctx.enter_context(nc.Block())

        XT = 0
        PL, PC, RG = 4096, 12288, 17408
        MR, MB, PR, PR2 = 17408, 18944, 20480, 21504
        CX, XN, JK = 4096, 6144, 8192
        BIAS, WP, WT = RG, RG + 4096, RG + 5120
        QDT, KDT = XT, XT + 2048
        XN2 = 2048
        XST, SALL, SEL, ACC = 4096, 8192, 12288, 13312
        SG, HID, HT2, YS, POS = 15360, 16064, 16768, 17536, 18560
        YB, JK2, ZT = RG, RG + 2048, RG + 3072
        QL, KL, VL, ZG, QB, BKV = 4096, 5120, 7168, 9216, 10240, 11264
        CIN, COUT = 12352, 13440
        QBT, KBT, KDUP, WP2, WT2, BTMP = 12352, 13376, 14400, 15424, 16448, 17472
        HTF, SGF, YF, JKF, ZTF = 4096, 9728, 11264, 13312, 14336
        U0, CV, SQ, MU = 4096, 6400, 8448, 10752
        E0 = 11264
        DL, DT_, DTT, DN, DC = E0, E0 + 1024, E0 + 2048, E0 + 3072, E0 + 4096
        VBG, KBG, UU, WW = E0 + 5120, E0 + 6144, E0 + 7168, E0 + 8192
        KTL, QDD, INT = E0 + 9216, E0 + 10240, E0 + 11264
        KTT, QTT, VNW, SST = 0, 1024, 2048, 2560
        TMPD = 3584

        MIX = [[R(PL + t * HALF, HALF), R(PL + 3 * D + t * HALF, HALF)] for t in range(TT)]
        MIX2 = [[R(DT_ + t * HALF, HALF), R(QB + t * HALF, HALF)] for t in range(TT)]

        GATES = [(PC + (2 + d) * D + t * HALF, PC + (2 * d + t) * HALF) for d in range(2) for t in range(TT)]
        GATES += [(PL + (4 + d) * D + t * HALF, PL + D + (2 * d + t) * HALF) for d in range(2) for t in range(TT)]

        def mod_rows(tag, at, n):
            if tag == "mod1":
                return R(MR + at, n)
            half, at = divmod(at, MODQ // 2)
            if half == 0:
                return rows[:, ROW_AT["logit0"][0] + at:ROW_AT["logit0"][0] + at + n]
            return consts[:, CONST_AT["after"][0] + at:CONST_AT["after"][0] + at + n]

        DIAGS, N_DIAGS = 16384, 8

        def diagonal(n):
            return R(DIAGS + n % N_DIAGS * P, P)

        def SBUF_STATE(d, i):
            return (WT if i == 0 else PC + 4 * D) + d * HALF

        def G_STATE(d):
            return R(TMPD if d == 0 else VL + 1024, HALF)

        DELTA_PASSES = [(1, 0), (1, 1), (0, 0), (0, 1)]

        def sm(at, n):
            return small[:, at:at + n]

        @block.tensor
        def _(pe):
            tally = Tally()
            fills = [0] * 8
            turn = [0]
            rotating = [ROTATING]
            n_freed = [0]

            def next_bank(tag, bank=None):
                if bank is None:
                    bank = turn[0] % rotating[0]
                    turn[0] += 1
                place[tag] = (bank, fills[bank])
                fills[bank] += 1
                return psum[:, bank, :]

            def frees(key, tag):
                if tag is None:
                    n_freed[0] += 1
                    freed_by[key] = (weights_used, n_freed[0])
                else:
                    freed_by[key] = (bank_filled[bank_of(tag)], nth(tag))

            def transpose(o, i):
                return nc.tensor.transpose(o, i, const("ident")[0:i.shape[0], 0:i.shape[0]])

            def transpose4(tag, tiles, rows_=P):
                bank = next_bank(tag)
                if nth(tag) > 1:
                    pe.wait_ge(bank_drained[bank_of(tag)], nth(tag) - 1)
                for i, a in enumerate(tiles):
                    ins = transpose(bank[0:a.shape[1], i * P:i * P + P], a)
                    if i == len(tiles) - 1:
                        ins.then_inc(bank_filled[bank_of(tag)], 1)

            def modulation(tag, cname):
                banks = [next_bank((tag, i)) for i in range(4)]
                for i in range(4):
                    if nth((tag, i)) > 1:
                        pe.wait_ge(bank_drained[bank_of((tag, i))], nth((tag, i)) - 1)
                stat = col(cname).rearrange("p (k m) -> p k m", k=KT)
                for k in range(KT):
                    for h in range(2):
                        enlist((tag, k, h))
                        pe.wait_ge(slot_loaded[slot_of((tag, k, h))], count_of[(tag, k, h)])
                        w = slot(slot_of((tag, k, h))).rearrange("p (j n) -> p j n", j=4)
                        for i in range(2):
                            for j in range(4):
                                ins = nc.tensor.matmul(banks[2 * h + i][32 * j:32 * j + 32, 0:384], stat[:, k, :],
                                                       w[:, j, i * 384:(i + 1) * 384], start=(k == 0),
                                                       stop=(k == KT - 1), skip_group_check=True)
                                if k == KT - 1 and j == 3:
                                    ins.then_inc(bank_filled[bank_of((tag, 2 * h + i))], 1)
                                elif i == 1 and j == 3:
                                    ins.then_inc(weights_used, 1)
                                if i == 1 and j == 3:
                                    frees((tag, k, h), (tag, 2 * h + i) if k == KT - 1 and j == 3 else None)
                for i in range(4):
                    pe.wait_ge(bank_drained[bank_of((tag, i))], nth((tag, i)))
                pe.wait_ge(consts_loaded, 16 * tally.due(consts_loaded))
                modulation_cols(tag)
                modulation_gates(tag)

            def modulation_part(tag, h, k, bank):
                if k == 0:
                    for i in range(2):
                        next_bank((tag, 2 * h + i), bank=bank + i)
                        if nth((tag, 2 * h + i)) > 1:
                            pe.wait_ge(bank_drained[bank_of((tag, 2 * h + i))], nth((tag, 2 * h + i)) - 1)
                enlist((tag, h, k))
                pe.wait_ge(slot_loaded[slot_of((tag, h, k))], count_of[(tag, h, k)])
                w = slot(slot_of((tag, h, k))).rearrange("p (j n) -> p j n", j=4)
                stat = col("c2").rearrange("p (k m) -> p k m", k=KT)[:, k, :]
                for i in range(2):
                    for j in range(4):
                        ins = nc.tensor.matmul(psum[32 * j:32 * j + 32, bank + i, 0:384], stat,
                                               w[:, j, i * 384:(i + 1) * 384], start=(k == 0), stop=(k == KT - 1),
                                               skip_group_check=True)
                        if k == KT - 1 and j == 3:
                            ins.then_inc(bank_filled[bank_of((tag, 2 * h + i))], 1)
                        elif i == 1 and j == 3:
                            ins.then_inc(weights_used, 1)
                        if i == 1 and j == 3:
                            frees((tag, h, k), (tag, 2 * h + i) if k == KT - 1 and j == 3 else None)

            def modulation_cols(tag):
                for j in range(4):
                    b = next_bank((tag, "cols", j))
                    if nth((tag, "cols", j)) > 1:
                        pe.wait_ge(bank_drained[bank_of((tag, "cols", j))], nth((tag, "cols", j)) - 1)
                    for m in range(12):
                        ins = nc.tensor.matmul(b[:, 2 * m:2 * m + 2], mod_rows(tag, m * P, P)[32 * j:32 * j + 2, :],
                                               const("ident")[32 * j:32 * j + 2, 32 * j:32 * j + 2], start=True,
                                               stop=True, skip_group_check=True)
                        if m == 11:
                            ins.then_inc(bank_filled[bank_of((tag, "cols", j))], 1)

            def modulation_gates(tag):
                for g in range(2):
                    for h in range(2):
                        j, off = divmod(2 * D + g * 3 * D + h * HALF, MODQ)
                        b = next_bank((tag, "gate", g, h))
                        if nth((tag, "gate", g, h)) > 1:
                            pe.wait_ge(bank_drained[bank_of((tag, "gate", g, h))], nth((tag, "gate", g, h)) - 1)
                        for u in range(2):
                            ins = nc.tensor.matmul(b[:, u * 256:(u + 1) * 256], const("first")[32 * j:32 * j + 2, :],
                                                    mod_rows(tag, off + u * 256, 256)[32 * j:32 * j + 2, :],
                                                   start=True, stop=True, skip_group_check=True)
                            if u == 1:
                                ins.then_inc(bank_filled[bank_of((tag, "gate", g, h))], 1)

            def normalised_T(tag, at):
                for t in range(TT):
                    pe.wait_ge(normed_ready if t == 0 else normed_second_ready,
                               tally.due(normed_ready if t == 0 else normed_second_ready))
                    for h in range(2):
                        transpose4((tag, t, h), [R(at + t * D + (4 * h + i) * P, P) for i in range(4)])

            def transposed(*tags):
                for tag in tags:
                    for t in range(TT):
                        for h in range(2):
                            pe.wait_ge(bank_drained[bank_of((tag, t, h))], nth((tag, t, h)))

            def project(tag, key, tiles, n, ctx_first=None):
                banks = {t: next_bank((tag, key, t)) for t in tiles}
                for t in tiles:
                    if nth((tag, key, t)) > 1:
                        pe.wait_ge(bank_drained[bank_of((tag, key, t))], nth((tag, key, t)) - 1)
                for h in range(2):
                    enlist((tag, key, h))
                    pe.wait_ge(slot_loaded[slot_of((tag, key, h))], count_of[(tag, key, h)])
                    w = slot(slot_of((tag, key, h)))[:, 0:4 * n].rearrange("p (k n) -> p k n", k=4)
                    for t in tiles:
                        for k in range(4):
                            kk = 4 * h + k
                            ins = nc.tensor.matmul(banks[t][:, 0:n], XTt(kk, t), w[:, k, :], start=(kk == 0),
                                                   stop=(kk == 7), skip_group_check=True)
                            if kk == 7:
                                ins.then_inc(bank_filled[bank_of((tag, key, t))], 1)
                            elif t == tiles[-1] and k == 3:
                                ins.then_inc(weights_used, 1)
                            if t == tiles[-1] and k == 3:
                                frees((tag, key, h), (tag, key, t) if kk == 7 else None)

            width = [512]

            def XTt(k, t):
                return R(XT + k * width[0] + t * P, P)

            def project_rows(tag, mixes):
                for t in range(TT):
                    pe.wait_ge(mix_ready, tally.due(mix_ready))
                    for h in range(2):
                        transpose4((tag, "T", t, h), [mixes[t][h][:, i * P:(i + 1) * P] for i in range(4)])
                for t in range(TT):
                    for h in range(2):
                        pe.wait_ge(bank_drained[bank_of((tag, "T", t, h))], nth((tag, "T", t, h)))
                width[0] = 256
                for c in range(2):
                    project(tag, c, range(TT), HALF)

            def attention(tag, n_steps, scores, values, between=None):
                for i in range(n_steps + 3):
                    if i < n_steps:
                        scores(i)
                        if between:
                            between(i)
                    if 2 <= i <= n_steps + 1:
                        pe.wait_ge(bank_drained[bank_of((tag, i - 2))], nth((tag, i - 2)))
                        transpose4((tag, "pT", i - 2), [R(PW[0] + i % 2 * HALF + c * P, P) for c in range(4)])
                    if i >= 3:
                        pe.wait_ge(bank_drained[bank_of((tag, "pT", i - 3))], nth((tag, "pT", i - 3)))
                        values(i - 3)

            PW = [WP]

            def ffn(n):
                for f in range(FT // 2):
                    for u in range(2):
                        b = next_bank((f"ffn{n}", f, u))
                        if nth((f"ffn{n}", f, u)) > 1:
                            pe.wait_ge(bank_drained[bank_of((f"ffn{n}", f, u))], nth((f"ffn{n}", f, u)) - 1)
                        if u == 0:
                            for h in range(2):
                                enlist((f"ffn{n}", f, h))
                                pe.wait_ge(slot_loaded[slot_of((f"ffn{n}", f, h))], count_of[(f"ffn{n}", f, h)])
                            ws = [slot(slot_of((f"ffn{n}", f, h)))[:, 0:2048].rearrange("p (k u n) -> p k u n", k=4,
                                                                                        u=2) for h in range(2)]
                        for i in range(2):
                            for k in range(KT):
                                ins = nc.tensor.matmul(b[:, i * 256:(i + 1) * 256],
                                                       ws[k // 4][:, k % 4, u, i * P:(i + 1) * P],
                                                       R(XT + k * 256, 256), start=(k == 0), stop=(k == 7),
                                                       skip_group_check=True)
                                if k == 7 and i == 1:
                                    ins.then_inc(bank_filled[bank_of((f"ffn{n}", f, u))], 1)
                                elif u == 1 and i == 1 and k % 4 == 3:
                                    ins.then_inc(weights_used, 1)
                                if u == 1 and i == 1 and k % 4 == 3:
                                    frees((f"ffn{n}", f, k // 4), (f"ffn{n}", f, u) if k == 7 and i == 1 else None)
                if n == 0:
                    pe.wait_ge(mod_rows_ready, tally.due(mod_rows_ready))
                    modulation_cols("mod2_1")
                banks = [next_bank((f"ffd{n}", t, c)) for t in range(TT) for c in range(2)]
                for t in range(TT):
                    for c in range(2):
                        if nth((f"ffd{n}", t, c)) > 1:
                            pe.wait_ge(bank_drained[bank_of((f"ffd{n}", t, c))], nth((f"ffd{n}", t, c)) - 1)
                for i in range((FT + 2) // 3):
                    enlist((f"ffd{n}", i))
                    pe.wait_ge(slot_loaded[slot_of((f"ffd{n}", i))], count_of[(f"ffd{n}", i)])
                    w = slot(slot_of((f"ffd{n}", i)))
                    for k in range(3 * i, min(3 * i + 3, FT)):
                        if k % 2 == 0:
                            pe.wait_ge(bank_drained[bank_of((f"ffn{n}", k // 2, 1))], nth((f"ffn{n}", k // 2, 1)))
                        for t in range(TT):
                            for c in range(2):
                                ins = nc.tensor.matmul(banks[2 * t + c], R(HTF + k * 256 + t * P, P),
                                                       w[:, (k % 3) * D + c * HALF:(k % 3) * D + (c + 1) * HALF],
                                                       start=(k == 0), stop=(k == FT - 1), skip_group_check=True)
                                if k == FT - 1:
                                    ins.then_inc(bank_filled[bank_of((f"ffd{n}", t, c))], 1)
                                elif (k % 3 == 2 or k == FT - 1) and t == c == 1:
                                    ins.then_inc(weights_used, 1)
                                if (k % 3 == 2 or k == FT - 1) and t == c == 1:
                                    frees((f"ffd{n}", i), (f"ffd{n}", t, c) if k == FT - 1 else None)

            pe.wait_ge(cond_ready, tally.due(cond_ready))
            modulation("mod1", "c1")
            normalised_T("x1", XN)
            normalised_T("ctx1", XN)
            transposed("x1", "ctx1")
            for c in range(8):
                project("in1", c, range(4) if c in (1, 2, 4, 5, 6) else range(2), HALF)
            pe.wait_ge(bank_drained[bank_of(("in1", 7, 1))], nth(("in1", 7, 1)))
            pe.wait_ge(bank_drained[bank_of(("in1", 6, 3))], nth(("in1", 6, 3)))
            for t in range(TT):
                transpose4(("qT", t), [R(PL + t * HALF + i * P, P) for i in range(4)])
                transpose4(("kcT", t), [R(PC + t * HALF + i * P, P) for i in range(4)])
            pe.wait_ge(rotated, tally.due(rotated, 2))
            for t in range(TT):
                transpose4(("qrT", t), [R(WT + t * HALF + i * P, P) for i in range(4)])
                transpose4(("krT", t), [R(PL + D + t * HALF + i * P, P) for i in range(4)])
            for t in range(TT):
                for kind in ("qT", "kcT", "qrT", "krT"):
                    pe.wait_ge(bank_drained[bank_of((kind, t))], nth((kind, t)))

            def qk(which, pair, at, n, base):
                return R(XT + which * 1024 + pair * 256 + at, n)[base:base + HEAD, :]

            def scores1(i):
                t, h = divmod(i, NA_HEADS)
                base = HEAD * (h % 2)
                b = next_bank(("na", i))
                if nth(("na", i)) > 1:
                    pe.wait_ge(bank_drained[bank_of(("na", i))], nth(("na", i)) - 1)
                nc.tensor.matmul(b[:, 0:256], qk(2, h // 2, t * P, P, base), qk(3, h // 2, 0, 256, base), start=True,
                                  stop=True, skip_group_check=True)
                ins = nc.tensor.matmul(b[:, 256:512], qk(0, h // 2, t * P, P, base), qk(1, h // 2, 0, 256, base),
                                       start=True, stop=True, skip_group_check=True)
                ins.then_inc(bank_filled[bank_of(("na", i))], 1)

            def values1(i):
                t, h = divmod(i, NA_HEADS)
                if h == 0:
                    next_bank(("nao", t), bank=6 + t)
                    if nth(("nao", t)) > 1:
                        pe.wait_ge(bank_drained[bank_of(("nao", t))], nth(("nao", t)) - 1)
                o = psum[:, 6 + t, h * HEAD:(h + 1) * HEAD]
                for c in range(4):
                    v = R((PL + 2 * D if c < 2 else PC + D) + (c % 2) * HALF + h * HEAD, HEAD)
                    ins = nc.tensor.matmul(o, R(WT + i % 2 * HALF + c * P, P), v, start=(c == 0), stop=(c == 3),
                                           skip_group_check=True)
                    if h == 7 and c == 3:
                        ins.then_inc(bank_filled[bank_of(("nao", t))], 1)
                    elif c == 3 and h < 7:
                        ins.then_inc(pv_done["na"], 1)

            def between_heads(i):
                if i % 2 == 0:
                    modulation_part("mod2_0", 0, i // 2, 4)

            rotating[0] = 4
            attention("na", TT * NA_HEADS, scores1, values1, between_heads)
            def ZC(d, t):
                return R(PC + (2 + d) * D + t * HALF, HALF)

            def ZL(d, t):
                return R(PL + (4 + d) * D + t * HALF, HALF)

            def KC(d, t):
                return R(PC + (2 * d + t) * HALF, HALF)

            def KLt(d, t):
                return R(PL + D + (2 * d + t) * HALF, HALF)

            for k in range(5):
                modulation_part("mod2_0", 1, k, 4)
            pe.wait_ge(log_forget_ready, tally.due(log_forget_ready, 8))
            for d in range(2):
                for t in range(TT):
                    b = next_bank(("hgc", d, t))
                    if nth(("hgc", d, t)) > 1:
                        pe.wait_ge(bank_drained[bank_of(("hgc", d, t))], nth(("hgc", d, t)) - 1)
                    whole = (1 - t if d == 0 else t)
                    ins = nc.tensor.matmul(b, const("after" if d == 0 else "before"), ZC(d, t), start=True,
                                           stop=not whole, skip_group_check=True)
                    if not whole:
                        ins.then_inc(bank_filled[bank_of(("hgc", d, t))], 1)
                    if whole:
                        ins = nc.tensor.matmul(b, const("ones"), ZC(d, 1 - t), start=False, stop=True,
                                               skip_group_check=True)
                        ins.then_inc(bank_filled[bank_of(("hgc", d, t))], 1)
            b = next_bank("decay")
            if nth("decay") > 1:
                pe.wait_ge(bank_drained[bank_of("decay")], nth("decay") - 1)
            for d in range(2):
                for t in range(TT):
                    for h in range(HG_HEADS):
                        at = ((d * 2 + t) * 4 + h) * 4
                        ins = nc.tensor.matmul(b[:, at:at + 4], ZL(d, t)[:, h * P:(h + 1) * P], const("chunk32"),
                                               start=True, stop=True, skip_group_check=True)
                        if at == 60:
                            ins.then_inc(bank_filled[bank_of("decay")], 1)
            for k in range(5, KT):
                modulation_part("mod2_0", 1, k, 4)
            pe.wait_ge(key_decayed, tally.due(key_decayed, 4))
            for d in range(2):
                b = next_bank(("hgs", d))
                if nth(("hgs", d)) > 1:
                    pe.wait_ge(bank_drained[bank_of(("hgs", d))], nth(("hgs", d)) - 1)
                for h in range(HG_HEADS):
                    for t in range(TT):
                        ins = nc.tensor.matmul(b[:, h * P:(h + 1) * P], KC(d, t)[:, h * P:(h + 1) * P],
                                               R(PC + 4 * D + t * HALF + h * P, P), start=(t == 0), stop=(t == 1),
                                               skip_group_check=True)
                        if h == 3 and t == 1:
                            ins.then_inc(bank_filled[bank_of(("hgs", d))], 1)
            for d in range(2):
                for t in range(TT):
                    for kind in ("pre32", "suf32"):
                        b = next_bank(("hg", kind, d, t))
                        if nth(("hg", kind, d, t)) > 1:
                            pe.wait_ge(bank_drained[bank_of(("hg", kind, d, t))], nth(("hg", kind, d, t)) - 1)
                        ins = nc.tensor.matmul(b, const(f"{kind}_{d}"), ZL(d, t), start=True, stop=True,
                                               skip_group_check=True)
                        ins.then_inc(bank_filled[bank_of(("hg", kind, d, t))], 1)
            for d in range(2):
                for t in range(TT):
                    pe.wait_ge(query_key_decayed, tally.due(query_key_decayed))
                    for which, at in ((0, BIAS), (1, BIAS + 2048)):
                        transpose4(("hgT", which, d, t), [R(at + (2 * d + t) * HALF + i * P, P) for i in range(4)])
            for d in range(2):
                for t in range(TT):
                    for which in range(2):
                        pe.wait_ge(bank_drained[bank_of(("hgT", which, d, t))], nth(("hgT", which, d, t)))
            for d in range(2):
                for t in range(TT):
                    b = next_bank(("hgA", d, t))
                    if nth(("hgA", d, t)) > 1:
                        pe.wait_ge(bank_drained[bank_of(("hgA", d, t))], nth(("hgA", d, t)) - 1)
                    for h in range(HG_HEADS):
                        ins = nc.tensor.matmul(b[:, h * P:(h + 1) * P], R(KDT + (2 * d + t) * HALF + h * P, P),
                                               R(QDT + (2 * d + t) * HALF + h * P, P), start=True, stop=True,
                                               skip_group_check=True)
                        if h == 3:
                            ins.then_inc(bank_filled[bank_of(("hgA", d, t))], 1)

            rotating[0] = ROTATING

            def IH(t):
                return R(PL + 6 * D + t * HALF, HALF)

            for d in range(2):
                for t in range(TT):
                    pe.wait_ge(bank_drained[bank_of(("hgA", d, t))], nth(("hgA", d, t)))
            for t in range(TT):
                next_bank(("hgo", t), bank=6 + t)
                if nth(("hgo", t)) > 1:
                    pe.wait_ge(bank_drained[bank_of(("hgo", t))], nth(("hgo", t)) - 1)
                for d in range(2):
                    for h in range(HG_HEADS):
                        nc.tensor.matmul(psum[:, 6 + t, h * P:(h + 1) * P],
                                         R(PC + 2 * D + (2 * d + t) * HALF + h * P, P), IH(t)[:, h * P:(h + 1) * P],
                                         start=(d == 0 and h == 0), stop=False, skip_group_check=True)
            for i in range(8):
                for d in range(2):
                    t, j = divmod(i if d == 0 else 7 - i, 4)
                    rows_ = slice(32 * j, 32 * j + 32)
                    if i < 7:
                        b = next_bank(("hgkv", i, d))
                        if nth(("hgkv", i, d)) > 1:
                            pe.wait_ge(bank_drained[bank_of(("hgkv", i, d))], nth(("hgkv", i, d)) - 1)
                        for h in range(HG_HEADS):
                            ins = nc.tensor.matmul(b[:, h * P:(h + 1) * P], KLt(d, t)[rows_, h * P:(h + 1) * P],
                                                   IH(t)[rows_, h * P:(h + 1) * P], start=True, stop=True,
                                                   skip_group_check=True)
                            if h == 3:
                                ins.then_inc(bank_filled[bank_of(("hgkv", i, d))], 1)
                for d in range(2):
                    t, j = divmod(i if d == 0 else 7 - i, 4)
                    pe.wait_ge(bank_drained[bank_of(("hgkv", i - 1, d) if i else ("hgs", d))],
                               nth(("hgkv", i - 1, d) if i else ("hgs", d)))
                    st = R(SBUF_STATE(d, i % 2), HALF)
                    for h in range(HG_HEADS):
                        last = h == 3
                        end = last and ((i == 7 and d == 1) or (i == 7 and d == 0))
                        ins = nc.tensor.matmul(psum[32 * j:32 * j + 32, 6 + t, h * P:(h + 1) * P],
                                               R(QDT + (2 * d + t) * HALF + h * P + 32 * j, 32),
                                               st[:, h * P:(h + 1) * P], start=False, stop=True,
                                               skip_group_check=True)
                        if end:
                            ins.then_inc(bank_filled[bank_of(("hgo", t))], 1)
                        elif last and not end:
                            ins.then_inc(hgrn_state_read, 1)
            project_rows("out1", MIX)
            normalised_T("x2", XN2)
            transposed("x2")
            b = next_bank("router")
            if nth("router") > 1:
                pe.wait_ge(bank_drained[bank_of("router")], nth("router") - 1)
            for t in range(TT):
                for k in range(KT):
                    ins = nc.tensor.matmul(b[:, t * 16:(t + 1) * 16], R(XT + k * 256 + t * P, P),
                                           col("w_router")[:, k * 16:(k + 1) * 16], start=(k == 0), stop=(k == 7),
                                           skip_group_check=True)
                    if t == 1 and k == 7:
                        ins.then_inc(bank_filled[bank_of("router")], 1)
            pe.wait_ge(affinity_ready, tally.due(affinity_ready))
            b = next_bank("affT")
            if nth("affT") > 1:
                pe.wait_ge(bank_drained[bank_of("affT")], nth("affT") - 1)
            for t in range(TT):
                ins = transpose(b[0:16, t * P:(t + 1) * P], sm(t * 16, 16))
                if t == 1:
                    ins.then_inc(bank_filled[bank_of("affT")], 1)
            pe.wait_ge(position_ready, tally.due(position_ready))
            b = next_bank("posT")
            if nth("posT") > 1:
                pe.wait_ge(bank_drained[bank_of("posT")], nth("posT") - 1)
            for t in range(TT):
                ins = transpose(b[:, t * 16:(t + 1) * 16], R(POS + 256, 256)[0:16, t * P:(t + 1) * P])
                if t == 1:
                    ins.then_inc(bank_filled[bank_of("posT")], 1)
            for e in range(0, N_EXPERTS, 2):
                b = next_bank(("posb", e))
                if nth(("posb", e)) > 1:
                    pe.wait_ge(bank_drained[bank_of(("posb", e))], nth(("posb", e)) - 1)
                for i in range(2):
                    ins = nc.tensor.matmul(b[:, i * 256:(i + 1) * 256],
                                           const("ident")[0:16, e + i:e + i + 1].to_broadcast([16, P]),
                                           R(POS + 256, 256)[0:16, :], start=True, stop=True, skip_group_check=True)
                    if i == 1:
                        ins.then_inc(bank_filled[bank_of(("posb", e))], 1)
            pe.wait_ge(selection_ready, tally.due(selection_ready, 2))
            for k in range(KT):
                b = next_bank(("xs", k))
                if nth(("xs", k)) > 1:
                    pe.wait_ge(bank_drained[bank_of(("xs", k))], nth(("xs", k)) - 1)
                for t in range(TT):
                    ins = nc.tensor.matmul(b, R(XN2 + t * D + k * P, P), R(SEL + t * HALF, HALF), start=(t == 0),
                                           stop=(t == 1), skip_group_check=True)
                    if t == 1:
                        ins.then_inc(bank_filled[bank_of(("xs", k))], 1)
            pe.wait_ge(bank_drained[bank_of(("posb", N_EXPERTS - 2))], nth(("posb", N_EXPERTS - 2)))
            for k in range(KT):
                pe.wait_ge(bank_drained[bank_of(("xs", k))], nth(("xs", k)))

            def combine(e):
                for half in range(2):
                    pe.wait_ge(bank_drained[bank_of(("y", e, half))], nth(("y", e, half)))
                for t in range(TT):
                    for c in range(2):
                        b = next_bank(("comb", e, t, c))
                        if nth(("comb", e, t, c)) > 1:
                            pe.wait_ge(bank_drained[bank_of(("comb", e, t, c))], nth(("comb", e, t, c)) - 1)
                        ins = nc.tensor.matmul(b, R(SALL + e * 256 + t * P, P), R(YS + c * HALF, HALF), start=True,
                                               stop=True, skip_group_check=True)
                        ins.then_inc(bank_filled[bank_of(("comb", e, t, c))], 1)

            for e in range(N_EXPERTS):
                banks = [[next_bank(("gu", e, u, c)) for c in range(2)] for u in range(2)]
                for u in range(2):
                    for c in range(2):
                        if nth(("gu", e, u, c)) > 1:
                            pe.wait_ge(bank_drained[bank_of(("gu", e, u, c))], nth(("gu", e, u, c)) - 1)
                for k in range(KT):
                    for u in range(2):
                        enlist(("expert", e, u, k))
                        pe.wait_ge(slot_loaded[slot_of(("expert", e, u, k))], count_of[("expert", e, u, k)])
                        w = slot(slot_of(("expert", e, u, k)))
                        for c in range(2):
                            for j in range(4):
                                ins = nc.tensor.matmul(banks[u][c][32 * j:32 * j + 32, 0:GCH],
                                                       R(XST + k * HALF + e * CAP, CAP), w[:,
                                                                                           j * COLG + c * GCH:j * COLG + (c + 1) * GCH],
                                                       start=(k == 0), stop=(k == 7), skip_group_check=True)
                                if k == 7 and j == 3:
                                    ins.then_inc(bank_filled[bank_of(("gu", e, u, c))], 1)
                                elif c == 1 and j == 3:
                                    ins.then_inc(weights_used, 1)
                                if c == 1 and j == 3:
                                    frees(("expert", e, u, k), ("gu", e, u, c) if k == 7 and j == 3 else None)
                if e:
                    combine(e - 1)
                if e == 2:
                    pe.wait_ge(mod_rows_ready, tally.due(mod_rows_ready))
                    modulation_cols("mod2_0")
                for c in range(2):
                    pe.wait_ge(bank_drained[bank_of(("gu", e, 1, c))], nth(("gu", e, 1, c)))
                b = next_bank(("hT", e, 0))
                if nth(("hT", e, 0)) > 1:
                    pe.wait_ge(bank_drained[bank_of(("hT", e, 0))], nth(("hT", e, 0)) - 1)
                for q in range(4):
                    ins = transpose(b[:, q * P:(q + 1) * P], R(HID, QMAIN * P).rearrange("p (r q) -> p q r",
                                                                                         q=QMAIN)[:, q, :])
                    if q == 3:
                        ins.then_inc(bank_filled[bank_of(("hT", e, 0))], 1)
                b = next_bank(("hT", e, 1))
                if nth(("hT", e, 1)) > 1:
                    pe.wait_ge(bank_drained[bank_of(("hT", e, 1))], nth(("hT", e, 1)) - 1)
                transpose(b[:, 0:P], R(HID, QMAIN * P).rearrange("p (r q) -> p q r", q=QMAIN)[:, 4, :])
                ins = transpose(b[0:TAIL, P:2 * P], R(HID + QMAIN * P, TAIL))
                ins.then_inc(bank_filled[bank_of(("hT", e, 1))], 1)
                for i in range(2):
                    pe.wait_ge(bank_drained[bank_of(("hT", e, i))], nth(("hT", e, i)))
                for half in range(2):
                    b = next_bank(("y", e, half))
                    if nth(("y", e, half)) > 1:
                        pe.wait_ge(bank_drained[bank_of(("y", e, half))], nth(("y", e, half)) - 1)
                    for j in range(4):
                        enlist(("down", e, half, j))
                        pe.wait_ge(slot_loaded[slot_of(("down", e, half, j))], count_of[("down", e, half, j)])
                    ws = [slot(slot_of(("down", e, half, j))).rearrange("p (q n) -> p q n", q=6) for j in range(4)]
                    for q in range(6):
                        n = P if q < QMAIN else TAIL
                        for j in range(4):
                            ins = nc.tensor.matmul(b[32 * j:32 * j + 32, :], R(HT2 + q * P + 32 * j, 32)[0:n, :],
                                                   ws[j][0:n, q, :], start=(q == 0), stop=(q == 5),
                                                   skip_group_check=True)
                            if q == 5 and j == 3:
                                ins.then_inc(bank_filled[bank_of(("y", e, half))], 1)
                            elif q == 5:
                                ins.then_inc(weights_used, 1)
                            if q == 5:
                                frees(("down", e, half, j), ("y", e, half) if q == 5 and j == 3 else None)
            combine(N_EXPERTS - 1)

            normalised_T("x3", XN)
            modulation_gates("mod2_0")
            normalised_T("ctx2", XN)
            transposed("x3", "ctx2")
            width[0] = 512
            for i in range(4):
                enlist(("qkv", i))
                pe.wait_ge(slot_loaded[slot_of(("qkv", i))], count_of[("qkv", i)])
                w = slot(slot_of(("qkv", i))).rearrange("p (k n) -> p k n", k=KT)
                for f in range(3):
                    ff = 3 * i + f
                    b = next_bank(("qkv", ff))
                    if nth(("qkv", ff)) > 1:
                        pe.wait_ge(bank_drained[bank_of(("qkv", ff))], nth(("qkv", ff)) - 1)
                    n = SEQ if ff < 4 else 2 * SEQ
                    for k in range(KT):
                        ins = nc.tensor.matmul(b[:, 0:n], w[:, k, f * P:(f + 1) * P], R(XT + k * 512, n),
                                               start=(k == 0), stop=(k == 7), skip_group_check=True)
                        if k == 7:
                            ins.then_inc(bank_filled[bank_of(("qkv", ff))], 1)
                        elif f == 2 and k == 7:
                            ins.then_inc(weights_used, 1)
                        if f == 2 and k == 7:
                            frees(("qkv", i), ("qkv", ff) if k == 7 else None)
                    if ff >= 2:
                        pe.wait_ge(short_conv_ready, tally.due(short_conv_ready))
                        transpose4(("qkvT", ff - 2), [R(COUT + ff % 2 * HALF + t * P, P)
                                                      for t in range(2 if ff - 2 < 4 else 4)])
            for ff in (10, 11):
                pe.wait_ge(short_conv_ready, tally.due(short_conv_ready))
                transpose4(("qkvT", ff), [R(COUT + ff % 2 * HALF + t * P, P) for t in range(4)])
            project("hyb", "z", range(2), 512)
            project("hyb", "q", range(2), 512)
            enlist(("hyb", "bkv"))
            pe.wait_ge(slot_loaded[slot_of(("hyb", "bkv"))], count_of[("hyb", "bkv")])
            w = slot(slot_of(("hyb", "bkv")))[:, 0:2176].rearrange("p (k n) -> p k n", k=KT)
            for t in range(4):
                b = next_bank(("bkv", t))
                if nth(("bkv", t)) > 1:
                    pe.wait_ge(bank_drained[bank_of(("bkv", t))], nth(("bkv", t)) - 1)
                for k in range(KT):
                    ins = nc.tensor.matmul(b[:, 0:272], XTt(k, t), w[:, k, :], start=(k == 0), stop=(k == 7),
                                           skip_group_check=True)
                    if k == 7:
                        ins.then_inc(bank_filled[bank_of(("bkv", t))], 1)
                    elif t == 3 and k == 7:
                        ins.then_inc(weights_used, 1)
                    if t == 3 and k == 7:
                        frees(("hyb", "bkv"), ("bkv", t) if k == 7 else None)
            pe.wait_ge(grouped_query_ready, tally.due(grouped_query_ready, 2))
            for t in range(TT):
                transpose4(("qbT", t), [R(QB + t * HALF + i * P, P) for i in range(4)])
            for g in range(2):
                if g == 0:
                    pe.wait_ge(grouped_key_ready, tally.due(grouped_key_ready, 4))
                transpose4(("kbT", g), [R(KDUP + t * 256 + g * P, P) for t in range(4)])
            for t in range(TT):
                pe.wait_ge(bank_drained[bank_of(("qbT", t))], nth(("qbT", t)))
                pe.wait_ge(bank_drained[bank_of(("kbT", t))], nth(("kbT", t)))

            def scores2(i):
                t, h = divmod(i, 8)
                base = HEAD * (h % 2)
                b = next_bank(("gq", i))
                if nth(("gq", i)) > 1:
                    pe.wait_ge(bank_drained[bank_of(("gq", i))], nth(("gq", i)) - 1)
                ins = nc.tensor.matmul(b, R(QBT + (h // 2) * 256 + t * P, P)[base:base + HEAD, :],
                                       R(KBT + (h // 4) * HALF, HALF)[base:base + HEAD, :], start=True, stop=True,
                                       skip_group_check=True)
                ins.then_inc(bank_filled[bank_of(("gq", i))], 1)

            def values2(i):
                t, h = divmod(i, 8)
                if h == 0:
                    next_bank(("gqo", t), bank=6 + t)
                    if nth(("gqo", t)) > 1:
                        pe.wait_ge(bank_drained[bank_of(("gqo", t))], nth(("gqo", t)) - 1)
                o = psum[:, 6 + t, h * HEAD:(h + 1) * HEAD]
                for c in range(4):
                    ins = nc.tensor.matmul(o, R(WT2 + i % 2 * HALF + c * P, P),
                                           R(BKV + c * 272 + 144 + (h // 4) * HEAD, HEAD), start=(c == 0),
                                           stop=(c == 3), skip_group_check=True)
                    if h == 7 and c == 3:
                        ins.then_inc(bank_filled[bank_of(("gqo", t))], 1)
                    elif c == 3 and h < 7:
                        ins.then_inc(pv_done["gq"], 1)

            PW[0] = WP2
            attention("gq", 16, scores2, values2)

            pe.wait_ge(log_decay_ready, tally.due(log_decay_ready))
            b = next_bank("gsums")
            if nth("gsums") > 1:
                pe.wait_ge(bank_drained[bank_of("gsums")], nth("gsums") - 1)
            b1 = next_bank("gsums1")
            if nth("gsums1") > 1:
                pe.wait_ge(bank_drained[bank_of("gsums1")], nth("gsums1") - 1)
            for t in range(4):
                for d in range(2):
                    at = t * 8 + d * 4
                    g = sm(64 + at, 4)
                    nc.tensor.matmul(b[:, at:at + 4], const(f"pre64_{d}"), g, start=True, stop=True,
                                     skip_group_check=True)
                    nc.tensor.matmul(b[:, 32 + at:36 + at], const(f"suf64_{d}"), g, start=True, stop=True,
                                     skip_group_check=True)
            for n in range(2):
                for t in range(4):
                    o = (b[:, 64 + t * 8:72 + t * 8], b1[:, t * 8:t * 8 + 8])[n]
                    ins = nc.tensor.matmul(o, const("ones")[64 * n:64 * n + 64, :],
                                           sm(64 + t * 8, 8)[64 * n:64 * n + 64, :], start=True, stop=True,
                                           skip_group_check=True)
                    if t == 3:
                        ins.then_inc(bank_filled[bank_of(("gsums", "gsums1")[n])], 1)
            pe.wait_ge(unit_qk_ready, tally.due(unit_qk_ready))
            for seg, d in DELTA_PASSES:
                lat = seg == 0
                if d == 0:
                    for t in range(TT):
                        tt = seg * 2 + t
                        transpose4(("kT", seg, t), [R(KL + tt * HALF + h * P, P) for h in range(4)])
                        if lat:
                            transpose4(("qTd", t), [R(QL + t * HALF + h * P, P) for h in range(4)])
                    for t in range(TT):
                        pe.wait_ge(bank_drained[bank_of(("kT", seg, t))], nth(("kT", seg, t)))
                        if lat:
                            pe.wait_ge(bank_drained[bank_of(("qTd", t))], nth(("qTd", t)))
                for t in range(TT):
                    pe.wait_ge(decay_rows_ready, tally.due(decay_rows_ready))
                    b = next_bank(("dec", seg, d, t))
                    if nth(("dec", seg, d, t)) > 1:
                        pe.wait_ge(bank_drained[bank_of(("dec", seg, d, t))], nth(("dec", seg, d, t)) - 1)
                    for h in range(4):
                        ins = nc.tensor.matmul(b[:, h * P:(h + 1) * P], R(DN + t * HALF + h * P, P),
                                               const(f"suf64_{d}"), start=True, stop=True, skip_group_check=True)
                        if h == 3:
                            ins.then_inc(bank_filled[bank_of(("dec", seg, d, t))], 1)
                    b = next_bank(("gram", seg, d, t))
                    if nth(("gram", seg, d, t)) > 1:
                        pe.wait_ge(bank_drained[bank_of(("gram", seg, d, t))], nth(("gram", seg, d, t)) - 1)
                    for h in range(4):
                        kt = R(KTT + t * HALF + h * P, P)
                        ins = nc.tensor.matmul(b[:, h * P:(h + 1) * P], kt, kt, start=True, stop=True,
                                               skip_group_check=True)
                        if h == 3:
                            ins.then_inc(bank_filled[bank_of(("gram", seg, d, t))], 1)
                if lat:
                    for t in range(TT):
                        pe.wait_ge(decay_cols_ready, tally.due(decay_cols_ready))
                        b = next_bank(("decT", d, t))
                        if nth(("decT", d, t)) > 1:
                            pe.wait_ge(bank_drained[bank_of(("decT", d, t))], nth(("decT", d, t)) - 1)
                        for h in range(4):
                            ins = nc.tensor.matmul(b[:, h * P:(h + 1) * P], R(DC + t * HALF + h * P, P),
                                                   const(f"pre64_{d}"), start=True, stop=True,
                                                   skip_group_check=True)
                            if h == 3:
                                ins.then_inc(bank_filled[bank_of(("decT", d, t))], 1)
                        b = next_bank(("kq", d, t))
                        if nth(("kq", d, t)) > 1:
                            pe.wait_ge(bank_drained[bank_of(("kq", d, t))], nth(("kq", d, t)) - 1)
                        for h in range(4):
                            ins = nc.tensor.matmul(b[:, h * P:(h + 1) * P], R(KTT + t * HALF + h * P, P),
                                                   R(QTT + t * HALF + h * P, P), start=True, stop=True,
                                                   skip_group_check=True)
                            if h == 3:
                                ins.then_inc(bank_filled[bank_of(("kq", d, t))], 1)
                        pe.wait_ge(query_decayed, tally.due(query_decayed))
                        transpose4(("qdT", d, t), [R(DTT + t * HALF + h * P, P) for h in range(4)])
                for lv in range(N_LEVELS):
                    for t in range(TT):
                        pe.wait_ge(coupling_ready, tally.due(coupling_ready))
                        if lv:
                            pe.wait_ge(bank_drained[bank_of(("n1" if lv == 1 else "tctT", seg, d, lv - 1, t))],
                                       nth(("n1" if lv == 1 else "tctT", seg, d, lv - 1, t)))
                        b = next_bank(("n1", seg, d, lv, t))
                        if nth(("n1", seg, d, lv, t)) > 1:
                            pe.wait_ge(bank_drained[bank_of(("n1", seg, d, lv, t))], nth(("n1", seg, d, lv, t)) - 1)
                        for h in range(4):
                            rhs = const("ident") if lv == 0 else R(DTT + t * HALF + h * P, P)
                            ins = nc.tensor.matmul(b[:, h * P:(h + 1) * P], R(DC + t * HALF + h * P, P), rhs,
                                                   start=True, stop=True, skip_group_check=True)
                            if h == 3:
                                ins.then_inc(bank_filled[bank_of(("n1", seg, d, lv, t))], 1)
                        if seg == 1 and 1 <= lv <= 4:
                            modulation_part("mod2_1", d, 2 * lv - 2 + t, 6)
                    if lv == 0:
                        continue
                    for t in range(TT):
                        pe.wait_ge(bank_drained[bank_of(("n1", seg, d, lv, t))], nth(("n1", seg, d, lv, t)))
                        if lv < N_LEVELS - 1:
                            b = next_bank(("tct", seg, d, lv, t))
                            if nth(("tct", seg, d, lv, t)) > 1:
                                pe.wait_ge(bank_drained[bank_of(("tct", seg, d, lv, t))],
                                           nth(("tct", seg, d, lv, t)) - 1)
                            for h in range(4):
                                ins = nc.tensor.matmul(b[:, h * P:(h + 1) * P], R(DN + t * HALF + h * P, P),
                                                       R(DT_ + t * HALF + h * P, P), start=True, stop=True,
                                                       skip_group_check=True)
                                if h == 3:
                                    ins.then_inc(bank_filled[bank_of(("tct", seg, d, lv, t))], 1)
                        b = next_bank(("tctT", seg, d, lv, t))
                        if nth(("tctT", seg, d, lv, t)) > 1:
                            pe.wait_ge(bank_drained[bank_of(("tctT", seg, d, lv, t))],
                                       nth(("tctT", seg, d, lv, t)) - 1)
                        for h in range(4):
                            ins = nc.tensor.matmul(b[:, h * P:(h + 1) * P], R(DT_ + t * HALF + h * P, P),
                                                   R(DN + t * HALF + h * P, P), start=True, stop=True,
                                                   skip_group_check=True)
                            if h == 3:
                                ins.then_inc(bank_filled[bank_of(("tctT", seg, d, lv, t))], 1)
                pe.wait_ge(kv_scaled, tally.due(kv_scaled, TT))
                for t in range(TT):
                    pe.wait_ge(bank_drained[bank_of(("tctT", seg, d, N_LEVELS - 1, t))],
                               nth(("tctT", seg, d, N_LEVELS - 1, t)))
                for t in range(TT):
                    b = next_bank(("u", seg, d, t))
                    if nth(("u", seg, d, t)) > 1:
                        pe.wait_ge(bank_drained[bank_of(("u", seg, d, t))], nth(("u", seg, d, t)) - 1)
                    for h in range(4):
                        ins = nc.tensor.matmul(b[:, h * P:(h + 1) * P], R(DTT + t * HALF + h * P, P),
                                               R(VBG + t * HALF + h * P, P), start=True, stop=True,
                                               skip_group_check=True)
                        if h == 3:
                            ins.then_inc(bank_filled[bank_of(("u", seg, d, t))], 1)
                    b = next_bank(("w", seg, d, t))
                    if nth(("w", seg, d, t)) > 1:
                        pe.wait_ge(bank_drained[bank_of(("w", seg, d, t))], nth(("w", seg, d, t)) - 1)
                    for h in range(4):
                        ins = nc.tensor.matmul(b[:, h * P:(h + 1) * P], R(KBG + t * HALF + h * P, P),
                                               R(DTT + t * HALF + h * P, P), start=True, stop=True,
                                               skip_group_check=True)
                        if h == 3:
                            ins.then_inc(bank_filled[bank_of(("w", seg, d, t))], 1)
                for t in range(TT):
                    pe.wait_ge(bank_drained[bank_of(("u", seg, d, t))], nth(("u", seg, d, t)))
                    pe.wait_ge(bank_drained[bank_of(("w", seg, d, t))], nth(("w", seg, d, t)))
                    if lat:
                        pe.wait_ge(bank_drained[bank_of(("qdT", d, t))], nth(("qdT", d, t)))
                for i in range(4):
                    t, n = divmod(i if d == 0 else 3 - i, 2)
                    r = slice(64 * n, 64 * n + 64)
                    st = R(SST + i % 2 * HALF, HALF)
                    if i == 0:
                        pe.wait_ge(delta_state_ready, tally.due(delta_state_ready))
                    else:
                        pe.wait_ge(bank_drained[bank_of(("dkv", seg, d, i - 1))], nth(("dkv", seg, d, i - 1)))
                    b = next_bank(("ws", seg, d, i))
                    if nth(("ws", seg, d, i)) > 1:
                        pe.wait_ge(bank_drained[bank_of(("ws", seg, d, i))], nth(("ws", seg, d, i)) - 1)
                    for h in range(4):
                        ins = nc.tensor.matmul(b[r, h * P:(h + 1) * P], R(WW + t * HALF + h * P + 64 * n, 64),
                                               st[:, h * P:(h + 1) * P], start=True, stop=True,
                                               skip_group_check=True)
                        if h == 3:
                            ins.then_inc(bank_filled[bank_of(("ws", seg, d, i))], 1)
                    if lat:
                        if d == 0 and n == 0:
                            next_bank(("dlo", t), bank=6 + t)
                            if nth(("dlo", t)) > 1:
                                pe.wait_ge(bank_drained[bank_of(("dlo", t))], nth(("dlo", t)) - 1)
                        o = psum[:, 6 + t, :]
                        for h in range(4):
                            nc.tensor.matmul(o[r, h * P:(h + 1) * P], R(QDD + t * HALF + h * P + 64 * n, 64),
                                             st[:, h * P:(h + 1) * P], start=(d == 0 and h == 0), stop=False,
                                             skip_group_check=True)
                    pe.wait_ge(bank_drained[bank_of(("ws", seg, d, i))], nth(("ws", seg, d, i)))
                    b = next_bank(("dkv", seg, d, i))
                    if nth(("dkv", seg, d, i)) > 1:
                        pe.wait_ge(bank_drained[bank_of(("dkv", seg, d, i))], nth(("dkv", seg, d, i)) - 1)
                    for h in range(4):
                        ins = nc.tensor.matmul(b[:, h * P:(h + 1) * P], R(KTL + t * HALF + h * P, P)[r, :],
                                               R(VNW + h * P, P)[r, :], start=True, stop=True,
                                               skip_group_check=True)
                        if h == 3:
                            ins.then_inc(bank_filled[bank_of(("dkv", seg, d, i))], 1)
                    if lat:
                        for h in range(4):
                            last = h == 3
                            end = last and d == 1 and n == 0
                            ins = nc.tensor.matmul(o[r, h * P:(h + 1) * P],
                                                   R(INT + t * HALF + h * P + 64 * n, 64)[r, :],
                                                   R(VNW + h * P, P)[r, :], start=False, stop=True,
                                                   skip_group_check=True)
                            if end:
                                ins.then_inc(bank_filled[bank_of(("dlo", t))], 1)
                            elif last and not end:
                                ins.then_inc(delta_out_added, 1)
            project_rows("out2", MIX2)
            normalised_T("f0", YF)
            transposed("f0")
            ffn(0)
            normalised_T("x4", YF)
            modulation_gates("mod2_1")
            transposed("x4")
            for f in range(KT // 2):
                for h in range(2):
                    enlist(("conf", f, h))
                    pe.wait_ge(slot_loaded[slot_of(("conf", f, h))], count_of[("conf", f, h)])
                ws = [slot(slot_of(("conf", f, h)))[:, 0:2048].rearrange("p (k u n) -> p k u n", k=4,
                                                                         u=2) for h in range(2)]
                for u in range(2):
                    b = next_bank(("conf", f, u))
                    if nth(("conf", f, u)) > 1:
                        pe.wait_ge(bank_drained[bank_of(("conf", f, u))], nth(("conf", f, u)) - 1)
                    for i in range(2):
                        for k in range(KT):
                            ins = nc.tensor.matmul(b[:, i * 256:(i + 1) * 256],
                                                   ws[k // 4][:, k % 4, u, i * P:(i + 1) * P], R(XT + k * 256, 256),
                                                   start=(k == 0), stop=(k == 7), skip_group_check=True)
                            if k == 7 and i == 1:
                                ins.then_inc(bank_filled[bank_of(("conf", f, u))], 1)
                            elif u == 1 and i == 1 and k % 4 == 3:
                                ins.then_inc(weights_used, 1)
                            if u == 1 and i == 1 and k % 4 == 3:
                                frees(("conf", f, k // 4), ("conf", f, u) if k == 7 and i == 1 else None)
            pe.wait_ge(bank_drained[bank_of(("conf", KT // 2 - 1, 0))], nth(("conf", KT // 2 - 1, 0)))
            b = next_bank("conv")
            if nth("conv") > 1:
                pe.wait_ge(bank_drained[bank_of("conv")], nth("conv") - 1)
            for i in range(2):
                for k in range(CONF_K):
                    pe.wait_ge(diag_ready, tally.due(diag_ready))
                    ft = KT - 2 + i
                    ins = nc.tensor.matmul(b[:, i * 256:(i + 1) * 256], diagonal(i * CONF_K + k),
                                           R(U0 + ft * UPAD + k, SEQ), start=(k == 0), stop=(k == CONF_K - 1),
                                           skip_group_check=True)
                    if i == 1 and k == CONF_K - 1:
                        ins.then_inc(bank_filled[bank_of("conv")], 1)
                    elif i == 0 or k < CONF_K - 1:
                        ins.then_inc(diag_used, 1)
            pe.wait_ge(bank_drained[bank_of("conv")], nth("conv"))
            for name, at, ready in (("mean", CV, conf_mean_in), ("var", SQ, conf_var_in)):
                pe.wait_ge(ready, tally.due(ready))
                b = next_bank(("conf", name))
                if nth(("conf", name)) > 1:
                    pe.wait_ge(bank_drained[bank_of(("conf", name))], nth(("conf", name)) - 1)
                for k in range(KT):
                    ins = nc.tensor.matmul(b[:, 0:256], const("ones"), R(at + k * 256, 256), start=(k == 0),
                                           stop=(k == 7), skip_group_check=True)
                    if k == 7:
                        ins.then_inc(bank_filled[bank_of(("conf", name))], 1)
            pe.wait_ge(conv_out_ready, tally.due(conv_out_ready, 8))
            for c in range(2):
                banks = {t: next_bank(("confo", c, t)) for t in range(TT)}
                for t in range(TT):
                    if nth(("confo", c, t)) > 1:
                        pe.wait_ge(bank_drained[bank_of(("confo", c, t))], nth(("confo", c, t)) - 1)
                for h in range(2):
                    enlist(("confo", c, h))
                    pe.wait_ge(slot_loaded[slot_of(("confo", c, h))], count_of[("confo", c, h)])
                    w = slot(slot_of(("confo", c, h)))[:, 0:2048].rearrange("p (k n) -> p k n", k=4)
                    for t in range(TT):
                        for k in range(4):
                            kk = 4 * h + k
                            ins = nc.tensor.matmul(banks[t], R(CV + kk * 256 + t * P, P), w[:, k, :],
                                                   start=(kk == 0), stop=(kk == 7), skip_group_check=True)
                            if kk == 7:
                                ins.then_inc(bank_filled[bank_of(("confo", c, t))], 1)
                            elif t == TT - 1 and k == 3:
                                ins.then_inc(weights_used, 1)
                            if t == TT - 1 and k == 3:
                                frees(("confo", c, h), ("confo", c, t) if kk == 7 else None)
            normalised_T("f1", YF)
            transposed("f1")
            ffn(1)

        @block.vector
        def _(v):
            tally = Tally()

            def bc(a, shape):
                return a.to_broadcast(shape)

            def modulation(tag, gp, gf, with_ctx):
                for i in range(4):
                    v.wait_ge(bank_filled[bank_of((tag, i))], nth((tag, i)))
                    ps = result((tag, i))
                    ins = v.tensor_tensor(R(MR + i * 384, 384), ps[:, 0:384], R(MB + i * 384, 384), ALU.add)
                    ins.then_inc(bank_drained[bank_of((tag, i))], 1)
                    v.wait_ge(bank_drained[bank_of((tag, i))], nth((tag, i)))
                modulation_cols(tag, gp, gf, with_ctx)
                modulation_gates(tag)

            def modulation_rows(tag, mb):
                v.wait_ge(mod_bias_loaded, 16 * tally.due(mod_bias_loaded, 2))
                for i in range(4):
                    v.wait_ge(bank_drained[bank_of((tag, i))], nth((tag, i)))
                    kept = mod_rows(tag, i * 384, 384)
                    ins = v.tensor_tensor(kept, kept, R(mb + i * 384, 384), ALU.add)
                    if i < 3:
                        ins.then_inc(vector_done, 1)
                        v.wait_ge(vector_done, tally.gave(vector_done))
                    else:
                        ins.then_inc(mod_rows_ready, 1)
                        v.wait_ge(mod_rows_ready, tally.gave(mod_rows_ready))

            def modulation_cols(tag, gp, gf, with_ctx):
                for j in range(4):
                    v.wait_ge(bank_filled[bank_of((tag, "cols", j))], nth((tag, "cols", j)))
                    ins = v.tensor_copy(modcol[:, 24 * j:24 * j + 24], result((tag, "cols", j))[:, 0:24])
                    ins.then_inc(bank_drained[bank_of((tag, "cols", j))], 1)
                    v.wait_ge(bank_drained[bank_of((tag, "cols", j))], nth((tag, "cols", j)))
                mc = modcol[:, :].rearrange("p (m c) -> p m c", c=2)
                if with_ctx:
                    ins = v.scalar_tensor_tensor(shsc[:, 16:24], mc[:, 8:16, 1], 1.0, col(gp), ALU.add, ALU.mult)
                    ins.then_inc(vector_done, 1)
                    v.wait_ge(vector_done, tally.gave(vector_done))
                ins = v.scalar_tensor_tensor(shsc[:, 0:8], mc[:, 8:16, 0], 1.0, col(gp), ALU.add, ALU.mult)
                ins.then_inc(vector_done, 1)
                v.wait_ge(vector_done, tally.gave(vector_done))
                ins = v.scalar_tensor_tensor(shsc[:, 8:16], mc[:, 32:40, 0], 1.0, col(gf), ALU.add, ALU.mult)
                ins.then_inc(mod_cols_ready, 1)
                v.wait_ge(mod_cols_ready, tally.gave(mod_cols_ready))

            def modulation_gates(tag):
                v.wait_ge(post_gains_loaded, 16 * tally.due(post_gains_loaded, 2))
                for g in range(2):
                    for h in range(2):
                        t = (tag, "gate", g, h)
                        v.wait_ge(bank_filled[bank_of(t)], nth(t))
                        ins = v.tensor_tensor(G[:, g, h * HALF:(h + 1) * HALF], result(t),
                                              R((PR if g == 0 else PR2) + h * HALF, HALF), ALU.mult)
                        ins.then_inc(bank_drained[bank_of(t)], 1)
                        v.wait_ge(bank_drained[bank_of(t)], nth(t))

            def rms_scale(n_sums, count, at_sum, at_r):
                ins = v.tensor_scalar(sm(at_r, n_sums), sm(at_sum, n_sums), 1.0 / count, EPS, ALU.mult, ALU.add)
                ins.then_inc(mean_square_ready, 1)
                v.wait_ge(mean_square_ready, tally.gave(mean_square_ready))
                v.wait_ge(root_ready, tally.due(root_ready))
                v.reciprocal(sm(at_r, n_sums), sm(at_r, n_sums)).then_inc(vector_done, 1)
                v.wait_ge(vector_done, tally.gave(vector_done))

            def normalise(src, at):
                for t in range(TT):
                    v.wait_ge(square_sum_ready, tally.due(square_sum_ready))
                ins = v.tensor_scalar(sm(712, TT), sm(710, TT), 1.0 / D, EPS, ALU.mult, ALU.add)
                ins.then_inc(mean_square_ready, 1)
                v.wait_ge(mean_square_ready, tally.gave(mean_square_ready))
                v.wait_ge(root_ready, tally.due(root_ready))
                v.reciprocal(sm(712, TT), sm(712, TT)).then_inc(rms_ready, 1)
                v.wait_ge(rms_ready, tally.gave(rms_ready))
                v.tensor_scalar(R(at, D), src[:, 0, :], sm(712, 1), None, ALU.mult).then_inc(normed_ready, 1)
                v.wait_ge(normed_ready, tally.gave(normed_ready))

            def modulated_T(tag, scale_at, shift_m, c, dst, wid, off):
                mc = modcol[:, :].rearrange("p (m c) -> p m c", c=2)
                for t in range(TT):
                    v.wait_ge(bank_filled[bank_of((tag, t, 0))], nth((tag, t, 0)))
                    ps = result((tag, t, 0))
                    for i in range(4):
                        ins = v.tensor_scalar(R(dst + i * wid + off + t * P, P), ps[:, i * P:(i + 1) * P],
                                              shsc[:, scale_at + i:scale_at + i + 1], mc[:, shift_m + i, c:c + 1],
                                              ALU.mult, ALU.add)
                        if i < 3:
                            ins.then_inc(vector_done, 1)
                            v.wait_ge(vector_done, tally.gave(vector_done))
                        else:
                            ins.then_inc(bank_drained[bank_of((tag, t, 0))], 1)
                            v.wait_ge(bank_drained[bank_of((tag, t, 0))], nth((tag, t, 0)))

            def post(fetch, at, zt, g, gives=x_ready):
                fetch()
                for t in range(TT):
                    v.wait_ge(square_sum_ready, tally.due(square_sum_ready))
                rms_scale(TT, D, 710, 712)
                for t in range(TT):
                    ins = v.scalar_tensor_tensor(R(zt, D), R(at + t * D, D), sm(712 + t, 1), G[:, g, :], ALU.mult,
                                                 ALU.mult)
                    ins.then_inc(vector_done, 1)
                    v.wait_ge(vector_done, tally.gave(vector_done))
                    v.tensor_tensor(X[:, t, :], X[:, t, :], R(zt, D), ALU.add).then_inc(gives, 1)
                    v.wait_ge(gives, tally.gave(gives))

            def post_psum(tags, zt, g, gives=x_ready):
                v.wait_ge(square_sum_ready, tally.due(square_sum_ready, 2 * TT))
                ins = v.tensor_reduce(sm(710, TT), sm(640, 2 * TT).rearrange("p (t c) -> p t c", t=TT), AX.X,
                                      ALU.add)
                ins.then_inc(vector_done, 1)
                v.wait_ge(vector_done, tally.gave(vector_done))
                rms_scale(TT, D, 710, 712)
                for t in range(TT):
                    for c in range(2):
                        tag = tags(t, c)
                        v.wait_ge(bank_filled[bank_of(tag)], nth(tag))
                        ins = v.scalar_tensor_tensor(R(zt + c * HALF, HALF), result(tag), sm(712 + t, 1),
                                                     G[:, g, c * HALF:(c + 1) * HALF], ALU.mult, ALU.mult)
                        ins.then_inc(bank_drained[bank_of(tag)], 1)
                        v.wait_ge(bank_drained[bank_of(tag)], nth(tag))
                    v.tensor_tensor(X[:, t, :], X[:, t, :], R(zt, D), ALU.add).then_inc(gives, 1)
                    v.wait_ge(gives, tally.gave(gives))

            def fetch_rows(tags, at, bias=None):
                def go():
                    for t in range(TT):
                        for c in range(2):
                            tag = tags(t, c)
                            dst = R(at + t * D + c * HALF, HALF)
                            if bias is None:
                                v.wait_ge(bank_filled[bank_of(tag)], nth(tag))
                                v.tensor_copy(dst, result(tag)).then_inc(bank_drained[bank_of(tag)], 1)
                                v.wait_ge(bank_drained[bank_of(tag)], nth(tag))
                            else:
                                v.wait_ge(bank_filled[bank_of(tag)], nth(tag))
                                ins = v.tensor_tensor(dst, result(tag), R(bias + c * HALF, HALF), ALU.add)
                                ins.then_inc(bank_drained[bank_of(tag)], 1)
                                v.wait_ge(bank_drained[bank_of(tag)], nth(tag))
                return go

            def rope(a, c, s, n_heads, tmp, to=None):
                to = a if to is None else to
                av = a.rearrange("p (h q r e) -> p h q r e", q=2, r=2, e=16)
                tv = tmp.rearrange("p (h q r e) -> p h q r e", q=2, r=2, e=16)
                sv = s.rearrange("p (q r e) -> p q r e", q=2, r=2)
                for r in range(2):
                    ins = v.tensor_tensor(tv[:, :, :, r, :], av[:, :, :, 1 - r, :],
                                          bc(sv[:, :, r, :].unsqueeze(1), [P, n_heads, 2, 16]), ALU.mult)
                    ins.then_inc(vector_done, 1)
                    v.wait_ge(vector_done, tally.gave(vector_done))
                a3 = a.rearrange("p (h e) -> p h e", h=n_heads)
                to3 = to.rearrange("p (h e) -> p h e", h=n_heads)
                v.tensor_tensor(to3, a3, bc(c.unsqueeze(1), [P, n_heads, HEAD]), ALU.mult).then_inc(vector_done, 1)
                v.wait_ge(vector_done, tally.gave(vector_done))
                return v.tensor_tensor(to, to, tmp, ALU.add)

            def attention(tag, bias, o_tag, outs):
                n = TT * 8
                for i in range(n + 2):
                    t, h = divmod(i, 8)
                    if i < n:
                        v.wait_ge(bank_filled[bank_of((tag, i))], nth((tag, i)))
                        ps = result((tag, i))
                        if bias:
                            ins = v.tensor_tensor(ps[:, 0:256], ps[:, 0:256], R(BIAS + i * 256, 256), ALU.add)
                            ins.then_inc(vector_done, 1)
                            v.wait_ge(vector_done, tally.gave(vector_done))
                        v.tensor_reduce(sm(600 + i % 8, 1), ps, AX.X, ALU.max, negate=True).then_inc(row_max, 1)
                        v.wait_ge(row_max, tally.gave(row_max))
                    if i >= 2:
                        j = i - 2
                        v.wait_ge(bank_filled[bank_of((tag, "pT", j))], nth((tag, "pT", j)))
                        ps = result((tag, "pT", j))
                        if j >= 2:
                            jt, jh = divmod(j - 2, 8)
                            if jh < 7:
                                v.wait_ge(pv_done[tag], tally.due(pv_done[tag]))
                            else:
                                v.wait_ge(bank_filled[bank_of((o_tag, jt))], nth((o_tag, jt)))
                        ins = v.tensor_copy(R((WT if bias else WT2) + j % 2 * HALF, HALF), ps)
                        ins.then_inc(bank_drained[bank_of((tag, "pT", j))], 1)
                        v.wait_ge(bank_drained[bank_of((tag, "pT", j))], nth((tag, "pT", j)))
                        if j % 8 == 7:
                            jt = j // 8
                            v.reciprocal(sm(616 + jt * 8, 8), sm(616 + jt * 8, 8)).then_inc(vector_done, 1)
                            v.wait_ge(vector_done, tally.gave(vector_done))
                            v.wait_ge(bank_filled[bank_of((o_tag, jt))], nth((o_tag, jt)))
                            ps = result((o_tag, jt))
                            ins = v.tensor_tensor(outs[jt].rearrange("p (h e) -> p h e", h=8),
                                                  ps.rearrange("p (h e) -> p h e", h=8), bc(sm(616 + jt * 8,
                                                                                               8).unsqueeze(2), [P,
                                                                                                                 8,
                                                                                                                 HEAD]),
                                                  ALU.mult)
                            ins.then_inc(bank_drained[bank_of((o_tag, jt))], 1)
                            v.wait_ge(bank_drained[bank_of((o_tag, jt))], nth((o_tag, jt)))

            def heads_ss(src, n_heads, wid, out_at):
                ins = v.tensor_reduce(sm(out_at, n_heads), src.rearrange("p (h e) -> p h e", h=n_heads), AX.X,
                                      ALU.add)
                ins.then_inc(vector_done, 1)
                v.wait_ge(vector_done, tally.gave(vector_done))

            def ffn(n):
                for f in range(FT // 2):
                    v.wait_ge(bank_drained[bank_of((f"ffn{n}", f, 0))], nth((f"ffn{n}", f, 0)))
                    v.wait_ge(bank_filled[bank_of((f"ffn{n}", f, 1))], nth((f"ffn{n}", f, 1)))
                    ps = result((f"ffn{n}", f, 1))
                    ins = v.tensor_tensor(R(HTF + f * 512, 512), R(SGF + f % 2 * 512, 512), ps, ALU.mult)
                    ins.then_inc(bank_drained[bank_of((f"ffn{n}", f, 1))], 1)
                    v.wait_ge(bank_drained[bank_of((f"ffn{n}", f, 1))], nth((f"ffn{n}", f, 1)))

            v.memset(R(MB, MODQ), 0.0).then_inc(mod_bias_zeroed, 1)
            v.wait_ge(mod_bias_zeroed, tally.gave(mod_bias_zeroed))
            v.wait_ge(consts_loaded, 16 * tally.due(consts_loaded))
            v.wait_ge(cols_loaded, 16 * tally.due(cols_loaded))
            v.wait_ge(rows_loaded, 16 * tally.due(rows_loaded))
            v.wait_ge(mod_bias_loaded, 16 * tally.due(mod_bias_loaded, 2))
            modulation("mod1", "g_pre1", "g_pre2", True)
            v.wait_ge(x_loaded, 16 * tally.due(x_loaded))
            normalise(X, XN)
            modulated_T("x1", 0, 0, 0, XT, 512, 0)
            v.wait_ge(bank_filled[bank_of(("x1", 1, 1))], nth(("x1", 1, 1)))
            v.wait_ge(ctx_loaded, 16 * tally.due(ctx_loaded))
            normalise(R(CX, 2048).rearrange("p (t n) -> p t n", t=TT), XN)
            modulated_T("ctx1", 16, 0, 1, XT, 512, 256)
            for c in range(8):
                for t in range(TT):
                    tag = ("in1", c, t)
                    v.wait_ge(bank_filled[bank_of(tag)], nth(tag))
                    ins = v.tensor_scalar(R(PL + c * D + t * HALF, HALF), result(tag),
                                          HEAD ** -0.5 if c == 0 else 1.0, None, ALU.mult)
                    ins.then_inc(bank_drained[bank_of(tag)], 1)
                    v.wait_ge(bank_drained[bank_of(tag)], nth(tag))
                if c < 2:
                    for t in range(TT):
                        a = R(PL + c * D + t * HALF, HALF)
                        ins = rope(a, const(f"cos{t}"), const(f"sin{t}"), NA_HEADS, R(WP, HALF),
                                   R(WT + t * HALF, HALF) if c == 0 else None)
                        if t == 1:
                            ins.then_inc(rotated, 1)
                            v.wait_ge(rotated, tally.gave(rotated))
                        else:
                            ins.then_inc(vector_done, 1)
                            v.wait_ge(vector_done, tally.gave(vector_done))
            v.wait_ge(bias_ready, tally.due(bias_ready))
            attention("na", True, "nao", [R(PL + t * HALF, HALF) for t in range(TT)])
            lb, oml = R(WP, HALF), R(WT, HALF)
            v.tensor_tensor(lb, row("logit0"), row("logit1"), ALU.subtract).then_inc(bound_in, 1)
            v.wait_ge(bound_in, tally.gave(bound_in))
            v.wait_ge(bound_ready, tally.due(bound_ready))
            v.tensor_scalar(oml, lb, -1.0, 1.0, ALU.mult, ALU.add).then_inc(vector_done, 1)
            v.wait_ge(vector_done, tally.gave(vector_done))

            for z_at, _k in GATES:
                z = R(z_at, HALF)
                v.wait_ge(sigmoid_ready, tally.due(sigmoid_ready))
                v.tensor_tensor(z, z, oml, ALU.mult).then_inc(vector_done, 1)
                v.wait_ge(vector_done, tally.gave(vector_done))
                v.tensor_tensor(z, z, lb, ALU.add).then_inc(forget_ready, 1)
                v.wait_ge(forget_ready, tally.gave(forget_ready))
            for d in range(2):
                for t in range(TT):
                    v.wait_ge(bank_drained[bank_of(("hgc", d, t))], nth(("hgc", d, t)))
                    k = R(PC + (2 * d + t) * HALF, HALF)
                    v.tensor_tensor(k, k, R(WP + (2 * d + t) % 2 * HALF, HALF), ALU.mult).then_inc(key_decayed, 1)
                    v.wait_ge(key_decayed, tally.gave(key_decayed))
            for d in range(2):
                v.wait_ge(bank_filled[bank_of(("hgs", d))], nth(("hgs", d)))
                ps = result(("hgs", d))
                v.tensor_copy(R(SBUF_STATE(d, 0), HALF), ps).then_inc(bank_drained[bank_of(("hgs", d))], 1)
                v.wait_ge(bank_drained[bank_of(("hgs", d))], nth(("hgs", d)))
            for d in range(2):
                for t in range(TT):
                    g = 2 * d + t
                    v.wait_ge(bank_drained[bank_of(("hg", "suf32", d, t))], nth(("hg", "suf32", d, t)))
                    k = R(PL + D + g * HALF, HALF)
                    q = R(PL + 3 * D + t * HALF, HALF)
                    qd, kd = R(BIAS + g * HALF, HALF), R(BIAS + 2048 + g * HALF, HALF)
                    v.tensor_tensor(qd, qd, q, ALU.mult).then_inc(vector_done, 1)
                    v.wait_ge(vector_done, tally.gave(vector_done))
                    v.tensor_tensor(kd, kd, k, ALU.mult).then_inc(vector_done, 1)
                    v.wait_ge(vector_done, tally.gave(vector_done))
                    v.tensor_tensor(k, k, R(WP + g % 2 * HALF, HALF), ALU.mult).then_inc(query_key_decayed, 1)
                    v.wait_ge(query_key_decayed, tally.gave(query_key_decayed))
            for d in range(2):
                for t in range(TT):
                    v.wait_ge(intra_zeroed, tally.due(intra_zeroed))
                    am = R(PC + 2 * D + (2 * d + t) * HALF, HALF).rearrange("p (h c) -> p h c", h=4)
                    tag = ("hgA", d, t)
                    mask = bc(const(f"pre32_{d}").bitcast(U32).unsqueeze(1), [P, 4, P])
                    v.wait_ge(bank_filled[bank_of(tag)], nth(tag))
                    ins = v.copy_predicated(am, mask, result(tag).rearrange("p (h c) -> p h c", h=4))
                    ins.then_inc(bank_drained[bank_of(tag)], 1)
                    v.wait_ge(bank_drained[bank_of(tag)], nth(tag))
            v.wait_ge(bank_drained[bank_of("decay")], nth("decay"))
            for i in range(7):
                for d in range(2):
                    t, j = divmod(i if d == 0 else 7 - i, 4)
                    old, new = R(SBUF_STATE(d, i % 2), HALF), R(SBUF_STATE(d, 1 - i % 2), HALF)
                    dec = sm(128 + ((d * 2 + t) * 4) * 4, 16).rearrange("p (h n) -> p h n", h=4)[:, :, j:j + 1]
                    if i >= 1:
                        v.wait_ge(hgrn_state_read, tally.due(hgrn_state_read))
                    ins = v.tensor_tensor(new.rearrange("p (h e) -> p h e", h=4),
                                          old.rearrange("p (h e) -> p h e", h=4), bc(dec, [P, 4, P]), ALU.mult)
                    ins.then_inc(vector_done, 1)
                    v.wait_ge(vector_done, tally.gave(vector_done))
                    v.wait_ge(bank_filled[bank_of(("hgkv", i, d))], nth(("hgkv", i, d)))
                    ins = v.tensor_tensor(new, new, result(("hgkv", i, d)), ALU.add)
                    ins.then_inc(bank_drained[bank_of(("hgkv", i, d))], 1)
                    v.wait_ge(bank_drained[bank_of(("hgkv", i, d))], nth(("hgkv", i, d)))

            def readout(o_tag, squares, gain, gate_tag, gate, outs):
                for t in range(TT):
                    v.wait_ge(squares_ready, tally.due(squares_ready))
                    heads_ss(squares[t], 4, P, 716 + t * 4)
                rms_scale(8, P, 716, 724)
                for t in range(TT):
                    o3 = outs[t].rearrange("p (h e) -> p h e", h=4)
                    tag = (o_tag, t)
                    v.wait_ge(bank_filled[bank_of(tag)], nth(tag))
                    ins = v.tensor_tensor(o3, result(tag).rearrange("p (h e) -> p h e", h=4),
                                          bc(sm(724 + 4 * t, 4).unsqueeze(2), [P, 4, P]), ALU.mult)
                    ins.then_inc(bank_drained[bank_of(tag)], 1)
                    v.wait_ge(bank_drained[bank_of(tag)], nth(tag))
                    v.tensor_tensor(o3, o3, bc(gain.unsqueeze(1), [P, 4, P]), ALU.mult).then_inc(vector_done, 1)
                    v.wait_ge(vector_done, tally.gave(vector_done))
                    v.wait_ge(gate_tag, tally.due(gate_tag))
                    v.tensor_tensor(outs[t], outs[t], gate[t], ALU.mult).then_inc(mix_ready, 1)
                    v.wait_ge(mix_ready, tally.gave(mix_ready))

            readout("hgo", [R(WP + t * HALF, HALF) for t in range(TT)], row("hg_norm"), hgrn_gate,
                    [R(PL + 7 * D + t * HALF, HALF) for t in range(TT)],
                    [R(PL + 3 * D + t * HALF, HALF) for t in range(TT)])

            def mix_T(tag):
                for t in range(TT):
                    v.wait_ge(bank_filled[bank_of((tag, "T", t, 0))], nth((tag, "T", t, 0)))
                    ps = result((tag, "T", t, 0))
                    dst = R(XT, 1024).rearrange("p (k n) -> p k n", k=4)[:, :, t * P:(t + 1) * P]
                    ins = v.tensor_copy(dst, ps.rearrange("p (k n) -> p k n", k=4))
                    ins.then_inc(bank_drained[bank_of((tag, "T", t, 0))], 1)
                    v.wait_ge(bank_drained[bank_of((tag, "T", t, 0))], nth((tag, "T", t, 0)))

            mix_T("out1")
            post_psum(lambda t, c: ("out1", c, t), ZT, 0)
            normalise(X, XN2)
            modulated_T("x2", 8, 24, 0, XT, 256, 0)
            v.wait_ge(bank_filled[bank_of("router")], nth("router"))
            ps = result("router")
            ins = v.tensor_reduce(sm(32, 2), ps[:, 0:32].rearrange("p (t e) -> p t e", t=2), AX.X, ALU.max,
                                  negate=True)
            ins.then_inc(vector_done, 1)
            v.wait_ge(vector_done, tally.gave(vector_done))
            for t in range(TT):
                ins = v.tensor_scalar(sm(t * 16, 16), ps[:, t * 16:(t + 1) * 16], sm(32 + t, 1), None, ALU.add)
                if t == 0:
                    ins.then_inc(vector_done, 1)
                    v.wait_ge(vector_done, tally.gave(vector_done))
                else:
                    ins.then_inc(bank_drained[bank_of("router")], 1)
                    v.wait_ge(bank_drained[bank_of("router")], nth("router"))
            v.wait_ge(affinity_exp, tally.due(affinity_exp))
            ins = v.tensor_reduce(sm(34, 2), sm(0, 32).rearrange("p (t e) -> p t e", t=2), AX.X, ALU.add)
            ins.then_inc(vector_done, 1)
            v.wait_ge(vector_done, tally.gave(vector_done))
            v.reciprocal(sm(34, 2), sm(34, 2)).then_inc(vector_done, 1)
            v.wait_ge(vector_done, tally.gave(vector_done))
            for t in range(TT):
                ins = v.tensor_scalar(sm(t * 16, 16), sm(t * 16, 16), sm(34 + t, 1), None, ALU.mult)
                if t == 0:
                    ins.then_inc(vector_done, 1)
                    v.wait_ge(vector_done, tally.gave(vector_done))
                else:
                    ins.then_inc(affinity_ready, 1)
                    v.wait_ge(affinity_ready, tally.gave(affinity_ready))
            W1, CS = R(POS, 256)[0:16, :], R(POS + 512, 256)[0:16, :]
            MK, PO = R(POS + 768, 256)[0:16, :], R(POS + 256, 256)[0:16, :]
            v.wait_ge(bank_filled[bank_of("affT")], nth("affT"))
            v.tensor_copy(W1, result("affT")[0:16, 0:256]).then_inc(bank_drained[bank_of("affT")], 1)
            v.wait_ge(bank_drained[bank_of("affT")], nth("affT"))
            for _i in range(CAP // 8):
                v.max(sm(40, 8)[0:16, :], W1).then_inc(vector_done, 1)
                v.wait_ge(vector_done, tally.gave(vector_done))
                v.match_replace(W1, sm(40, 8)[0:16, :], W1, -1.0).then_inc(vector_done, 1)
                v.wait_ge(vector_done, tally.gave(vector_done))
            v.tensor_scalar(MK, W1, 0.0, None, ALU.is_lt).then_inc(vector_done, 1)
            v.wait_ge(vector_done, tally.gave(vector_done))
            v.memset(PO, 0.0).then_inc(vector_done, 1)
            v.wait_ge(vector_done, tally.gave(vector_done))
            v.tensor_tensor_scan(CS, MK, PO, 0.0, ALU.add, ALU.add).then_inc(vector_done, 1)
            v.wait_ge(vector_done, tally.gave(vector_done))
            v.tensor_tensor(CS, CS, MK, ALU.mult).then_inc(vector_done, 1)
            v.wait_ge(vector_done, tally.gave(vector_done))
            v.tensor_scalar(PO, CS, -1.0, None, ALU.add).then_inc(position_ready, 1)
            v.wait_ge(position_ready, tally.gave(position_ready))
            v.wait_ge(bank_filled[bank_of("posT")], nth("posT"))
            v.tensor_copy(sm(48, 32), result("posT")[:, 0:32]).then_inc(bank_drained[bank_of("posT")], 1)
            v.wait_ge(bank_drained[bank_of("posT")], nth("posT"))
            for t in range(TT):
                ins = v.tensor_tensor(R(SEL + t * HALF, HALF).rearrange("p (e s) -> p e s", e=16),
                                      bc(const("iota").unsqueeze(1), [P, 16, CAP]),
                                      bc(sm(48 + t * 16, 16).unsqueeze(2), [P, 16, CAP]), ALU.is_equal)
                ins.then_inc(selection_ready, 1)
                v.wait_ge(selection_ready, tally.gave(selection_ready))
            for e in range(0, N_EXPERTS, 2):
                v.wait_ge(bank_filled[bank_of(("posb", e))], nth(("posb", e)))
                ins = v.tensor_scalar(R(SALL + e * 256, 512), result(("posb", e)), const("slot"), None,
                                      ALU.is_equal)
                ins.then_inc(bank_drained[bank_of(("posb", e))], 1)
                v.wait_ge(bank_drained[bank_of(("posb", e))], nth(("posb", e)))
            mc = modcol[:, :].rearrange("p (m c) -> p m c", c=2)
            for k in range(KT):
                v.wait_ge(bank_filled[bank_of(("xs", k))], nth(("xs", k)))
                ins = v.tensor_scalar(R(XST + k * HALF, HALF), result(("xs", k)), shsc[:, 8 + k:9 + k],
                                      mc[:, 24 + k, 0:1], ALU.mult, ALU.add)
                ins.then_inc(bank_drained[bank_of(("xs", k))], 1)
                v.wait_ge(bank_drained[bank_of(("xs", k))], nth(("xs", k)))

            def combine(e):
                for t in range(TT):
                    for c in range(2):
                        tag = ("comb", e, t, c)
                        acc, aff = R(ACC + t * D + c * HALF, HALF), sm(t * 16 + e, 1)
                        if e == 0:
                            v.wait_ge(bank_filled[bank_of(tag)], nth(tag))
                            ins = v.tensor_scalar(acc, result(tag), aff, None, ALU.mult)
                            ins.then_inc(bank_drained[bank_of(tag)], 1)
                            v.wait_ge(bank_drained[bank_of(tag)], nth(tag))
                        else:
                            v.wait_ge(bank_filled[bank_of(tag)], nth(tag))
                            ins = v.scalar_tensor_tensor(acc, result(tag), aff, acc, ALU.mult, ALU.add)
                            ins.then_inc(bank_drained[bank_of(tag)], 1)
                            v.wait_ge(bank_drained[bank_of(tag)], nth(tag))

            v.memset(R(XT, MODQ), 0.0).then_inc(mod_bias_zeroed, 1)
            v.wait_ge(mod_bias_zeroed, tally.gave(mod_bias_zeroed))
            for e in range(N_EXPERTS):
                for c in range(2):
                    v.wait_ge(bank_drained[bank_of(("gu", e, 0, c))], nth(("gu", e, 0, c)))
                    tag = ("gu", e, 1, c)
                    v.wait_ge(bank_filled[bank_of(tag)], nth(tag))
                    ins = v.tensor_tensor(R(HID + c * GCH, GCH), R(SG + c * GCH, GCH), result(tag)[:, 0:GCH],
                                          ALU.mult)
                    ins.then_inc(bank_drained[bank_of(tag)], 1)
                    v.wait_ge(bank_drained[bank_of(tag)], nth(tag))
                if e:
                    combine(e - 1)
                if e == 2:
                    modulation_rows("mod2_0", XT)
                    modulation_cols("mod2_0", "g_mix0", "g_ffn0", True)
                v.wait_ge(bank_filled[bank_of(("hT", e, 0))], nth(("hT", e, 0)))
                ps = result(("hT", e, 0))
                v.tensor_copy(R(HT2, 512), ps).then_inc(bank_drained[bank_of(("hT", e, 0))], 1)
                v.wait_ge(bank_drained[bank_of(("hT", e, 0))], nth(("hT", e, 0)))
                v.wait_ge(bank_filled[bank_of(("hT", e, 1))], nth(("hT", e, 1)))
                ps = result(("hT", e, 1))
                v.tensor_copy(R(HT2 + 512, P), ps[:, 0:P]).then_inc(vector_done, 1)
                v.wait_ge(vector_done, tally.gave(vector_done))
                ins = v.tensor_copy(R(HT2 + 640, P)[0:TAIL, :], ps[0:TAIL, P:2 * P])
                ins.then_inc(bank_drained[bank_of(("hT", e, 1))], 1)
                v.wait_ge(bank_drained[bank_of(("hT", e, 1))], nth(("hT", e, 1)))
            combine(N_EXPERTS - 1)

            post(lambda: None, ACC, ZT, 1)

            normalise(X, XN)
            modulated_T("x3", 0, 0, 0, XT, 512, 0)
            modulation_gates("mod2_0")
            v.wait_ge(bank_filled[bank_of(("x3", 1, 1))], nth(("x3", 1, 1)))
            v.wait_ge(ctx_loaded, 16 * tally.due(ctx_loaded))
            normalise(R(CX, 2048).rearrange("p (t n) -> p t n", t=TT), XN)
            modulated_T("ctx2", 16, 0, 1, XT, 512, 256)
            v.wait_ge(bank_filled[bank_of(("ctx2", 1, 1))], nth(("ctx2", 1, 1)))
            v.memset(R(CIN, 4 * PADW), 0.0).then_inc(vector_done, 1)
            v.wait_ge(vector_done, tally.gave(vector_done))
            v.memset(R(COUT, 1024), 0.0).then_inc(pads_zeroed, 1)
            v.wait_ge(pads_zeroed, tally.gave(pads_zeroed))

            def conv_in(i):
                return R(CIN + i % 2 * 2 * PADW, 2 * PADW).rearrange("p (s n) -> p s n", s=2)

            for ff in range(12):
                v.wait_ge(bank_drained[bank_of(("qkv", ff))], nth(("qkv", ff)))
                n = 1 if ff < 4 else 2
                src = conv_in(ff)[:, 0:n, :]
                dst = R(COUT + ff % 2 * HALF, HALF).rearrange("p (s n) -> p s n", s=2)[:, 0:n, :]
                if ff >= 2:
                    v.wait_ge(bank_filled[bank_of(("qkvT", ff - 2))], nth(("qkvT", ff - 2)))
                w = col("conv_w")
                ins = v.tensor_scalar(dst, src[:, :, 0:SEQ], w[:, ff * SHORT_K:ff * SHORT_K + 1], None, ALU.mult)
                ins.then_inc(vector_done, 1)
                v.wait_ge(vector_done, tally.gave(vector_done))
                for k in range(1, SHORT_K):
                    ins = v.scalar_tensor_tensor(dst, src[:, :, k:k + SEQ], w[:, ff * SHORT_K + k:ff * SHORT_K + k + 1],
                                                 dst, ALU.mult, ALU.add)
                    if k < SHORT_K - 1:
                        ins.then_inc(vector_done, 1)
                        v.wait_ge(vector_done, tally.gave(vector_done))
                    else:
                        ins.then_inc(short_conv_sum, 1)
                        v.wait_ge(short_conv_sum, tally.gave(short_conv_sum))
            tmp = R(BTMP, HALF)
            v.wait_ge(bank_drained[bank_of(("qkvT", 7))], nth(("qkvT", 7)))
            groups = [R(QL + t * HALF, HALF) for t in range(2)] + [R(KL + t * HALF, HALF) for t in range(4)]
            for i, a in enumerate(groups):
                v.tensor_tensor(tmp, a, a, ALU.mult).then_inc(vector_done, 1)
                v.wait_ge(vector_done, tally.gave(vector_done))
                heads_ss(tmp, 4, P, 716 + 4 * i)
            rms_scale(24, 1.0, 716, 576)
            v.tensor_scalar(sm(576, 8), sm(576, 8), P ** -0.5, None, ALU.mult).then_inc(vector_done, 1)
            v.wait_ge(vector_done, tally.gave(vector_done))
            for i, a in enumerate(groups):
                a3 = a.rearrange("p (h e) -> p h e", h=4)
                ins = v.tensor_tensor(a3, a3, bc(sm(576 + 4 * i, 4).unsqueeze(2), [P, 4, P]), ALU.mult)
                if i < 5:
                    ins.then_inc(vector_done, 1)
                    v.wait_ge(vector_done, tally.gave(vector_done))
                else:
                    ins.then_inc(unit_qk_ready, 1)
                    v.wait_ge(unit_qk_ready, tally.gave(unit_qk_ready))
            for t in range(TT):
                v.wait_ge(bank_filled[bank_of(("hyb", "z", t))], nth(("hyb", "z", t)))
                ins = v.tensor_copy(R(ZG + t * HALF, HALF), result(("hyb", "z", t)))
                ins.then_inc(bank_drained[bank_of(("hyb", "z", t))], 1)
                v.wait_ge(bank_drained[bank_of(("hyb", "z", t))], nth(("hyb", "z", t)))
            for t in range(TT):
                v.wait_ge(bank_filled[bank_of(("hyb", "q", t))], nth(("hyb", "q", t)))
                ins = v.tensor_copy(R(QB + t * HALF, HALF), result(("hyb", "q", t)))
                ins.then_inc(bank_drained[bank_of(("hyb", "q", t))], 1)
                v.wait_ge(bank_drained[bank_of(("hyb", "q", t))], nth(("hyb", "q", t)))
            for t in range(TT):
                q = R(QB + t * HALF, HALF)
                v.tensor_tensor(tmp, q, q, ALU.mult).then_inc(vector_done, 1)
                v.wait_ge(vector_done, tally.gave(vector_done))
                heads_ss(tmp, 8, HEAD, 716 + 8 * t)
            rms_scale(16, HEAD, 716, 576)
            for t in range(TT):
                q = R(QB + t * HALF, HALF)
                q3 = q.rearrange("p (h e) -> p h e", h=8)
                ins = v.tensor_tensor(q3, q3, bc(sm(576 + 8 * t, 8).unsqueeze(2), [P, 8, HEAD]), ALU.mult)
                ins.then_inc(vector_done, 1)
                v.wait_ge(vector_done, tally.gave(vector_done))
                ins = v.tensor_tensor(q3, q3, bc(row("q_norm").unsqueeze(1), [P, 8, HEAD]), ALU.mult)
                ins.then_inc(vector_done, 1)
                v.wait_ge(vector_done, tally.gave(vector_done))
                rope(q, const(f"cos{t}"), const(f"sin{t}"), 8, tmp).then_inc(vector_done, 1)
                v.wait_ge(vector_done, tally.gave(vector_done))
                v.tensor_scalar(q, q, HEAD ** -0.5, None, ALU.mult).then_inc(grouped_query_ready, 1)
                v.wait_ge(grouped_query_ready, tally.gave(grouped_query_ready))
            for t in range(4):
                v.wait_ge(bank_filled[bank_of(("bkv", t))], nth(("bkv", t)))
                ins = v.tensor_copy(R(BKV + t * 272, 272), result(("bkv", t))[:, 0:272])
                ins.then_inc(bank_drained[bank_of(("bkv", t))], 1)
                v.wait_ge(bank_drained[bank_of(("bkv", t))], nth(("bkv", t)))
            v.wait_ge(bank_drained[bank_of(("qkvT", 11))], nth(("qkvT", 11)))
            for t in range(4):
                k = R(BKV + t * 272 + 16, P)
                v.tensor_tensor(tmp[:, 0:P], k, k, ALU.mult).then_inc(vector_done, 1)
                v.wait_ge(vector_done, tally.gave(vector_done))
                heads_ss(tmp[:, 0:P], 2, HEAD, 732 + 2 * t)
            rms_scale(8, HEAD, 732, 592)
            for t in range(4):
                k = R(BKV + t * 272 + 16, P)
                k3 = k.rearrange("p (h e) -> p h e", h=2)
                ins = v.tensor_tensor(k3, k3, bc(sm(592 + 2 * t, 2).unsqueeze(2), [P, 2, HEAD]), ALU.mult)
                ins.then_inc(vector_done, 1)
                v.wait_ge(vector_done, tally.gave(vector_done))
                ins = v.tensor_tensor(k3, k3, bc(row("k_norm").unsqueeze(1), [P, 2, HEAD]), ALU.mult)
                ins.then_inc(vector_done, 1)
                v.wait_ge(vector_done, tally.gave(vector_done))
                if t < 2:
                    rope(k, const(f"cos{t}"), const(f"sin{t}"), 2, tmp[:, 0:P]).then_inc(vector_done, 1)
                    v.wait_ge(vector_done, tally.gave(vector_done))
                dup = R(KDUP + t * 256, 256).rearrange("p (h r e) -> p h r e", h=2, r=2)
                v.tensor_copy(dup, bc(k3.unsqueeze(2), [P, 2, 2, HEAD])).then_inc(grouped_key_ready, 1)
                v.wait_ge(grouped_key_ready, tally.gave(grouped_key_ready))
            ba = R(BKV, 4 * 272).rearrange("p (t n) -> p t n", t=4)
            x8 = ba[:, :, 8:16]

            def s4(at):
                return sm(at, 32).rearrange("p (t n) -> p t n", t=4)

            ins = v.tensor_tensor(s4(64), x8, bc(row("dt_bias").unsqueeze(1), [P, 4, 8]), ALU.add)
            ins.then_inc(vector_done, 1)
            v.wait_ge(vector_done, tally.gave(vector_done))
            v.tensor_scalar(s4(96), s4(64), -1.0, None, ALU.mult).then_inc(vector_done, 1)
            v.wait_ge(vector_done, tally.gave(vector_done))
            v.tensor_tensor(s4(96), s4(96), s4(64), ALU.min).then_inc(vector_done, 1)
            v.wait_ge(vector_done, tally.gave(vector_done))
            v.tensor_scalar(s4(64), s4(64), 0.0, None, ALU.max).then_inc(softplus_in, 1)
            v.wait_ge(softplus_in, tally.gave(softplus_in))
            v.wait_ge(softplus_exp, tally.due(softplus_exp))
            v.tensor_scalar(sm(96, 32), sm(96, 32), 1.0, None, ALU.add).then_inc(softplus_one, 1)
            v.wait_ge(softplus_one, tally.gave(softplus_one))
            v.wait_ge(softplus_log, tally.due(softplus_log))
            v.tensor_tensor(sm(64, 32), sm(64, 32), sm(96, 32), ALU.add).then_inc(vector_done, 1)
            v.wait_ge(vector_done, tally.gave(vector_done))
            ins = v.tensor_tensor(s4(64), s4(64), bc(sm(160, 8).unsqueeze(1), [P, 4, 8]), ALU.mult)
            ins.then_inc(vector_done, 1)
            v.wait_ge(vector_done, tally.gave(vector_done))
            v.tensor_scalar(sm(64, 32), sm(64, 32), -1.0, None, ALU.mult).then_inc(log_decay_ready, 1)
            v.wait_ge(log_decay_ready, tally.gave(log_decay_ready))
            attention("gq", False, "gqo", [R(QB + t * HALF, HALF) for t in range(TT)])
            v.wait_ge(bank_drained[bank_of("gsums1")], nth("gsums1"))
            for seg, d in DELTA_PASSES:
                lat = seg == 0
                if d == 0:
                    for t in range(TT):
                        v.wait_ge(bank_filled[bank_of(("kT", seg, t))], nth(("kT", seg, t)))
                        ins = v.tensor_copy(R(KTT + t * HALF, HALF), result(("kT", seg, t)))
                        ins.then_inc(bank_drained[bank_of(("kT", seg, t))], 1)
                        v.wait_ge(bank_drained[bank_of(("kT", seg, t))], nth(("kT", seg, t)))
                        if lat:
                            v.wait_ge(bank_filled[bank_of(("qTd", t))], nth(("qTd", t)))
                            ins = v.tensor_copy(R(QTT + t * HALF, HALF), result(("qTd", t)))
                            ins.then_inc(bank_drained[bank_of(("qTd", t))], 1)
                            v.wait_ge(bank_drained[bank_of(("qTd", t))], nth(("qTd", t)))

                def per_head(vec):
                    return bc(vec.unsqueeze(2), [P, 4, P])

                def h3(at):
                    return R(at, HALF).rearrange("p (h e) -> p h e", h=4)

                for t in range(TT):
                    at = (seg * 2 + t) * 8 + d * 4
                    g = sm(64 + at, 4)
                    ins = v.tensor_tensor(h3(DN + t * HALF), bc(const(f"pre64_{d}").unsqueeze(1), [P, 4, P]),
                                          per_head(g), ALU.mult)
                    ins.then_inc(decay_rows_ready, 1)
                    v.wait_ge(decay_rows_ready, tally.gave(decay_rows_ready))
                for t in range(TT):
                    at = (seg * 2 + t) * 8 + d * 4
                    v.wait_ge(bank_drained[bank_of(("dec", seg, d, t))], nth(("dec", seg, d, t)))
                    tag = ("gram", seg, d, t)
                    ins = v.tensor_tensor(h3(DL + t * HALF), h3(DL + t * HALF), per_head(sm(224 + at, 4)), ALU.mult)
                    ins.then_inc(vector_done, 1)
                    v.wait_ge(vector_done, tally.gave(vector_done))
                    v.wait_ge(bank_filled[bank_of(tag)], nth(tag))
                    ins = v.tensor_tensor(R(DL + t * HALF, HALF), R(DL + t * HALF, HALF), result(tag), ALU.mult)
                    ins.then_inc(bank_drained[bank_of(tag)], 1)
                    v.wait_ge(bank_drained[bank_of(tag)], nth(tag))
                if lat:
                    for t in range(TT):
                        at = t * 8 + d * 4
                        ins = v.tensor_tensor(h3(DC + t * HALF), bc(const(f"suf64_{d}").unsqueeze(1), [P, 4, P]),
                                              per_head(sm(64 + at, 4)), ALU.mult)
                        ins.then_inc(decay_cols_ready, 1)
                        v.wait_ge(decay_cols_ready, tally.gave(decay_cols_ready))
                        v.wait_ge(bank_drained[bank_of(("decT", d, t))], nth(("decT", d, t)))
                        tag = ("kq", d, t)
                        ins = v.tensor_tensor(h3(INT + t * HALF), h3(INT + t * HALF),
                                              bc(const(f"pre64_{d}").unsqueeze(1), [P, 4, P]), ALU.mult)
                        ins.then_inc(vector_done, 1)
                        v.wait_ge(vector_done, tally.gave(vector_done))
                        v.wait_ge(bank_filled[bank_of(tag)], nth(tag))
                        ins = v.tensor_tensor(R(INT + t * HALF, HALF), R(INT + t * HALF, HALF), result(tag),
                                              ALU.mult)
                        ins.then_inc(bank_drained[bank_of(tag)], 1)
                        v.wait_ge(bank_drained[bank_of(tag)], nth(tag))
                        ins = v.tensor_tensor(h3(DTT + t * HALF), h3(QL + t * HALF), per_head(sm(256 + at, 4)),
                                              ALU.mult)
                        ins.then_inc(query_decayed, 1)
                        v.wait_ge(query_decayed, tally.gave(query_decayed))
                        tag = ("qdT", d, t)
                        v.wait_ge(bank_filled[bank_of(tag)], nth(tag))
                        v.tensor_copy(R(QDD + t * HALF, HALF), result(tag)).then_inc(bank_drained[bank_of(tag)], 1)
                        v.wait_ge(bank_drained[bank_of(tag)], nth(tag))
                ident4 = bc(const("ident").unsqueeze(1), [P, 4, P])
                for lv in range(N_LEVELS):
                    if lv == 0:
                        for t in range(TT):
                            tag = ("n1", seg, d, lv, t)
                            v.wait_ge(bank_filled[bank_of(tag)], nth(tag))
                            n1 = result(tag).rearrange("p (h e) -> p h e", h=4)
                            ins = v.tensor_tensor(h3(DT_ + t * HALF), ident4, h3(DC + t * HALF), ALU.subtract)
                            ins.then_inc(vector_done, 1)
                            v.wait_ge(vector_done, tally.gave(vector_done))
                            ins = v.tensor_tensor(h3(DTT + t * HALF), ident4, n1, ALU.subtract)
                            ins.then_inc(bank_drained[bank_of(tag)], 1)
                            v.wait_ge(bank_drained[bank_of(tag)], nth(tag))
                        continue
                    for t in range(TT):
                        ta, tb = ("tct", seg, d, lv, t), ("tctT", seg, d, lv, t)
                        v.wait_ge(bank_filled[bank_of(tb)], nth(tb))
                        ps = result(tb)
                        if lv < N_LEVELS - 1:
                            v.wait_ge(bank_filled[bank_of(ta)], nth(ta))
                            ins = v.tensor_tensor(R(DT_ + t * HALF, HALF), R(DT_ + t * HALF, HALF), result(ta),
                                                  ALU.subtract)
                            ins.then_inc(bank_drained[bank_of(ta)], 1)
                            v.wait_ge(bank_drained[bank_of(ta)], nth(ta))
                        ins = v.tensor_tensor(R(DTT + t * HALF, HALF), R(DTT + t * HALF, HALF), ps, ALU.subtract)
                        ins.then_inc(bank_drained[bank_of(tb)], 1)
                        v.wait_ge(bank_drained[bank_of(tb)], nth(tb))
                for t in range(TT):
                    v.wait_ge(bank_filled[bank_of(("u", seg, d, t))], nth(("u", seg, d, t)))
                    ins = v.tensor_copy(R(UU + t * HALF, HALF), result(("u", seg, d, t)))
                    ins.then_inc(bank_drained[bank_of(("u", seg, d, t))], 1)
                    v.wait_ge(bank_drained[bank_of(("u", seg, d, t))], nth(("u", seg, d, t)))
                if seg == 1:
                    v.memset(R(SST, HALF), 0.0).then_inc(delta_state_ready, 1)
                    v.wait_ge(delta_state_ready, tally.gave(delta_state_ready))
                else:
                    v.tensor_copy(R(SST, HALF), G_STATE(d)).then_inc(delta_state_ready, 1)
                    v.wait_ge(delta_state_ready, tally.gave(delta_state_ready))
                for i in range(4):
                    t, n = divmod(i if d == 0 else 3 - i, 2)
                    r = slice(64 * n, 64 * n + 64)
                    old, new = R(SST + i % 2 * HALF, HALF), R(SST + (1 - i % 2) * HALF, HALF)
                    if lat and i >= 1:
                        if (d, i) == (1, 2):
                            v.wait_ge(bank_filled[bank_of(("dlo", 1))], nth(("dlo", 1)))
                        else:
                            v.wait_ge(delta_out_added, tally.due(delta_out_added))
                    tag = ("ws", seg, d, i)
                    v.wait_ge(bank_filled[bank_of(tag)], nth(tag))
                    ins = v.tensor_tensor(R(VNW, HALF)[r, :], R(UU + t * HALF, HALF)[r, :], result(tag)[r, :],
                                          ALU.subtract)
                    ins.then_inc(bank_drained[bank_of(tag)], 1)
                    v.wait_ge(bank_drained[bank_of(tag)], nth(tag))
                    el = sm(320 + n * 32 + (seg * 2 + t) * 8 + d * 4, 4)
                    ins = v.tensor_tensor(new.rearrange("p (h e) -> p h e", h=4),
                                          old.rearrange("p (h e) -> p h e", h=4), per_head(el), ALU.mult)
                    ins.then_inc(vector_done, 1)
                    v.wait_ge(vector_done, tally.gave(vector_done))
                    tag = ("dkv", seg, d, i)
                    dst = G_STATE(d) if seg == 1 and i == 3 else new
                    v.wait_ge(bank_filled[bank_of(tag)], nth(tag))
                    v.tensor_tensor(dst, new, result(tag), ALU.add).then_inc(bank_drained[bank_of(tag)], 1)
                    v.wait_ge(bank_drained[bank_of(tag)], nth(tag))
                if lat and d == 0:
                    v.wait_ge(delta_out_added, tally.due(delta_out_added))
            readout("dlo", [R(DL + t * HALF, HALF) for t in range(TT)], row("out_norm"), delta_gate,
                    [R(ZG + t * HALF, HALF) for t in range(TT)], [R(E0 + 1024 + t * HALF, HALF) for t in range(TT)])
            mix_T("out2")
            post_psum(lambda t, c: ("out2", c, t), ZTF, 0)
            normalise(X, YF)
            modulated_T("f0", 8, 24, 0, XT, 256, 0)
            v.memset(R(MB, MODQ), 0.0).then_inc(mod_bias_zeroed, 1)
            v.wait_ge(mod_bias_zeroed, tally.gave(mod_bias_zeroed))
            ffn(0)
            modulation_rows("mod2_1", MB)
            modulation_cols("mod2_1", "g_mix1", "g_ffn1", False)
            post_psum(lambda t, c: ("ffd0", t, c), ZTF, 1)
            normalise(X, YF)
            modulated_T("x4", 0, 0, 0, XT, 256, 0)
            modulation_gates("mod2_1")
            v.memset(R(U0, KT * UPAD), 0.0).then_inc(vector_done, 1)
            v.wait_ge(vector_done, tally.gave(vector_done))

            def U(f):
                return R(U0 + f * UPAD, UPAD)

            w = col("conf_dw_w")
            def gated_pair(f):
                v.wait_ge(bank_drained[bank_of(("conf", f, 1))], nth(("conf", f, 1)))
                v.wait_ge(bank_filled[bank_of(("conf", f, 0))], nth(("conf", f, 0)))
                ps = result(("conf", f, 0))
                for i in range(2):
                    ins = v.scalar_tensor_tensor(U(2 * f + i)[:, CONF_K // 2:CONF_K // 2 + SEQ],
                                                 ps[:, i * 256:(i + 1) * 256], col("conf_b_in")[:, 2 * f + i:2 * f + i + 1],
                                                 R(SGF + f % 2 * 512 + i * 256, 256), ALU.add, ALU.mult)
                    if i == 0:
                        ins.then_inc(vector_done, 1)
                        v.wait_ge(vector_done, tally.gave(vector_done))
                    else:
                        ins.then_inc(bank_drained[bank_of(("conf", f, 0))], 1)
                        v.wait_ge(bank_drained[bank_of(("conf", f, 0))], nth(("conf", f, 0)))

            for f in range(KT // 2 - 1):
                gated_pair(f)
                if f == KT // 2 - 2:
                    gated_pair(f + 1)
                for k in range(CONF_K):
                    for ft in (2 * f, 2 * f + 1):
                        dst, src = R(CV + ft * 256, 256), U(ft)[:, k:k + SEQ]
                        wk = w[:, ft * CONF_K + k:ft * CONF_K + k + 1]
                        if k == 0:
                            ins = v.tensor_scalar(dst, src, wk, col("conf_dw_b")[:, ft:ft + 1], ALU.mult, ALU.add)
                        else:
                            ins = v.scalar_tensor_tensor(dst, src, wk, dst, ALU.mult, ALU.add)
                        if k == CONF_K - 1 and ft == KT - 3:
                            ins.then_inc(conf_mean_in, 1)
                            v.wait_ge(conf_mean_in, tally.gave(conf_mean_in))
                        else:
                            ins.then_inc(vector_done, 1)
                            v.wait_ge(vector_done, tally.gave(vector_done) - 1)
            v.wait_ge(vector_done, tally.given[vector_done])
            mu, r_ = R(MU, 256), R(MU + 256, 256)
            v.wait_ge(bank_filled[bank_of(("conf", "mean"))], nth(("conf", "mean")))
            ins = v.tensor_scalar(mu, result(("conf", "mean"))[:, 0:256], 1.0 / D, None, ALU.mult)
            ins.then_inc(bank_drained[bank_of(("conf", "mean"))], 1)
            v.wait_ge(bank_drained[bank_of(("conf", "mean"))], nth(("conf", "mean")))
            cv3 = R(CV, 2048).rearrange("p (f n) -> p f n", f=KT)
            v.tensor_tensor(cv3, cv3, bc(mu.unsqueeze(1), [P, KT, 256]), ALU.subtract).then_inc(centred_ready, 1)
            v.wait_ge(centred_ready, tally.gave(centred_ready))
            v.wait_ge(bank_filled[bank_of(("conf", "var"))], nth(("conf", "var")))
            ins = v.tensor_scalar(r_, result(("conf", "var"))[:, 0:256], 1.0 / D, EPS, ALU.mult, ALU.add)
            ins.then_inc(bank_drained[bank_of(("conf", "var"))], 1)
            v.wait_ge(bank_drained[bank_of(("conf", "var"))], nth(("conf", "var")))
            v.wait_ge(root_ready, tally.due(root_ready))
            v.reciprocal(r_, r_).then_inc(vector_done, 1)
            v.wait_ge(vector_done, tally.gave(vector_done))
            v.tensor_tensor(cv3, cv3, bc(r_.unsqueeze(1), [P, KT, 256]), ALU.mult).then_inc(layer_norm_ready, 1)
            v.wait_ge(layer_norm_ready, tally.gave(layer_norm_ready))
            v.wait_ge(out_bias_loaded, 16 * tally.due(out_bias_loaded))
            post(fetch_rows(lambda t, c: ("confo", c, t), YF, bias=E0 + 4096), YF, ZTF, 0)
            normalise(X, YF)
            modulated_T("f1", 8, 24, 0, XT, 256, 0)
            ffn(1)
            post_psum(lambda t, c: ("ffd1", t, c), ZTF, 1, gives=out_ready)

        @block.scalar
        def _(a):
            tally = Tally()

            def root(at):
                a.wait_ge(mean_square_ready, tally.due(mean_square_ready))
                a.activation(at, at, ACT.Sqrt).then_inc(root_ready, 1)
                a.wait_ge(root_ready, tally.gave(root_ready))

            def sum_rows(src, jk, rows_of=None):
                for t in range(TT):
                    for c in range(2 if rows_of else 0):
                        a.wait_ge(bank_drained[bank_of(rows_of(t, c))], nth(rows_of(t, c)))
                    ins = a.activation(R(jk, D), src(t), ACT.Square, accum_out=sm(710 + t, 1))
                    ins.then_inc(square_sum_ready, 1)
                    a.wait_ge(square_sum_ready, tally.gave(square_sum_ready))
                root(sm(712, TT))

            def normalise(src, jk, at):
                sum_rows(src, jk)
                a.wait_ge(rms_ready, tally.due(rms_ready))
                a.activation(R(at + D, D), src(1), ACT.Identity, scale=sm(713, 1)).then_inc(normed_second_ready, 1)
                a.wait_ge(normed_second_ready, tally.gave(normed_second_ready))

            def sum_psum(jk, rows_of):
                for t in range(TT):
                    for c in range(2):
                        a.wait_ge(bank_filled[bank_of(rows_of(t, c))], nth(rows_of(t, c)))
                        ins = a.activation(R(jk, HALF), result(rows_of(t, c)), ACT.Square,
                                           accum_out=sm(640 + 2 * t + c, 1))
                        ins.then_inc(square_sum_ready, 1)
                        a.wait_ge(square_sum_ready, tally.gave(square_sum_ready))
                root(sm(712, TT))

            def modulated_T(tag, scale_at, shift_m, c, dst, wid, off):
                mc = modcol[:, :].rearrange("p (m c) -> p m c", c=2)
                for t in range(TT):
                    a.wait_ge(bank_filled[bank_of((tag, t, 1))], nth((tag, t, 1)))
                    ps = result((tag, t, 1))
                    for i in range(4):
                        k = 4 + i
                        ins = a.activation(R(dst + k * wid + off + t * P, P), ps[:, i * P:(i + 1) * P], ACT.Identity,
                                           bias=mc[:, shift_m + k, c:c + 1], scale=shsc[:, scale_at + k:scale_at + k + 1])
                        if i < 3:
                            ins.then_inc(scalar_done, 1)
                            a.wait_ge(scalar_done, tally.gave(scalar_done))
                        else:
                            ins.then_inc(bank_drained[bank_of((tag, t, 1))], 1)
                            a.wait_ge(bank_drained[bank_of((tag, t, 1))], nth((tag, t, 1)))

            def attention(tag, wp):
                for i in range(16):
                    a.wait_ge(row_max, tally.due(row_max))
                    a.wait_ge(bank_filled[bank_of((tag, i))], nth((tag, i)))
                    ps = result((tag, i))
                    if i >= 2:
                        a.wait_ge(bank_filled[bank_of((tag, "pT", i - 2))], nth((tag, "pT", i - 2)))
                    ins = a.activation(R(wp + i % 2 * HALF, HALF), ps, ACT.Exp, bias=sm(600 + i % 8, 1),
                                       accum_out=sm(616 + i, 1))
                    ins.then_inc(bank_drained[bank_of((tag, i))], 1)
                    a.wait_ge(bank_drained[bank_of((tag, i))], nth((tag, i)))

            def ffn(n):
                for f in range(FT // 2):
                    if f >= 2:
                        a.wait_ge(bank_drained[bank_of((f"ffn{n}", f - 2, 1))], nth((f"ffn{n}", f - 2, 1)))
                    give_ = ("ffn" + str(n), f, 0)
                    a.wait_ge(bank_filled[bank_of(give_)], nth(give_))
                    ins = a.activation(R(SGF + f % 2 * 512, 512), result(give_), ACT.Silu)
                    ins.then_inc(bank_drained[bank_of(give_)], 1)
                    a.wait_ge(bank_drained[bank_of(give_)], nth(give_))

            def keep_rows(tag, h):
                for i in (2 * h, 2 * h + 1):
                    a.wait_ge(bank_filled[bank_of((tag, i))], nth((tag, i)))
                    ins = a.copy(mod_rows(tag, i * 384, 384), result((tag, i))[:, 0:384])
                    ins.then_inc(bank_drained[bank_of((tag, i))], 1)
                    a.wait_ge(bank_drained[bank_of((tag, i))], nth((tag, i)))

            def mix_T(tag):
                for t in range(TT):
                    a.wait_ge(bank_filled[bank_of((tag, "T", t, 1))], nth((tag, "T", t, 1)))
                    ps = result((tag, "T", t, 1))
                    dst = R(XT + 1024, 1024).rearrange("p (k n) -> p k n", k=4)[:, :, t * P:(t + 1) * P]
                    ins = a.copy(dst, ps.rearrange("p (k n) -> p k n", k=4))
                    ins.then_inc(bank_drained[bank_of((tag, "T", t, 1))], 1)
                    a.wait_ge(bank_drained[bank_of((tag, "T", t, 1))], nth((tag, "T", t, 1)))

            a.wait_ge(cols_loaded, 16 * tally.due(cols_loaded))
            a.activation(col("c1"), col("c1"), ACT.Silu).then_inc(scalar_done, 1)
            a.wait_ge(scalar_done, tally.gave(scalar_done))
            a.activation(col("c2"), col("c2"), ACT.Silu).then_inc(cond_ready, 1)
            a.wait_ge(cond_ready, tally.gave(cond_ready))
            a.wait_ge(rows_loaded, 16 * tally.due(rows_loaded))
            a.wait_ge(x_loaded, 16 * tally.due(x_loaded))
            normalise(lambda t: X[:, t, :], JK, XN)
            a.wait_ge(mod_cols_ready, tally.due(mod_cols_ready))
            modulated_T("x1", 0, 0, 0, XT, 512, 0)
            a.wait_ge(ctx_loaded, 16 * tally.due(ctx_loaded))
            normalise(lambda t: R(CX + t * D, D), JK, XN)
            modulated_T("ctx1", 16, 0, 1, XT, 512, 256)
            for i, c in enumerate((1, 2, 4, 5, 6)):
                for t in range(2, 4):
                    tag = ("in1", c, t)
                    a.wait_ge(bank_filled[bank_of(tag)], nth(tag))
                    ins = a.copy(R(PC + i * D + (t - 2) * HALF, HALF), result(tag))
                    ins.then_inc(bank_drained[bank_of(tag)], 1)
                    a.wait_ge(bank_drained[bank_of(tag)], nth(tag))
            for t in range(TT):
                for tag, which in ((("qT", t), 0), (("kcT", t), 1)):
                    dst = R(XT + which * 1024, 1024).rearrange("p (i n) -> p i n", i=4)[:, :, t * P:(t + 1) * P]
                    a.wait_ge(bank_filled[bank_of(tag)], nth(tag))
                    ins = a.copy(dst, result(tag).rearrange("p (i n) -> p i n", i=4))
                    ins.then_inc(bank_drained[bank_of(tag)], 1)
                    a.wait_ge(bank_drained[bank_of(tag)], nth(tag))
            for t in range(TT):
                for tag, which in ((("qrT", t), 2), (("krT", t), 3)):
                    dst = R(XT + which * 1024, 1024).rearrange("p (i n) -> p i n", i=4)[:, :, t * P:(t + 1) * P]
                    a.wait_ge(bank_filled[bank_of(tag)], nth(tag))
                    ins = a.copy(dst, result(tag).rearrange("p (i n) -> p i n", i=4))
                    ins.then_inc(bank_drained[bank_of(tag)], 1)
                    a.wait_ge(bank_drained[bank_of(tag)], nth(tag))
            attention("na", WP)
            a.wait_ge(bound_in, tally.due(bound_in))
            keep_rows("mod2_0", 0)
            a.activation(R(WP, HALF), R(WP, HALF), ACT.Sigmoid).then_inc(bound_ready, 1)
            a.wait_ge(bound_ready, tally.gave(bound_ready))
            groups = [R(PC + (2 + d) * D + t * HALF, HALF) for d in range(2) for t in range(TT)]
            groups += [R(PL + (4 + d) * D + t * HALF, HALF) for d in range(2) for t in range(TT)]
            for z in groups:
                a.activation(z, z, ACT.Sigmoid).then_inc(sigmoid_ready, 1)
                a.wait_ge(sigmoid_ready, tally.gave(sigmoid_ready))
            for t in range(TT):
                g = R(PL + 7 * D + t * HALF, HALF)
                a.activation(g, g, ACT.Sigmoid).then_inc(hgrn_gate, 1)
                a.wait_ge(hgrn_gate, tally.gave(hgrn_gate))
            for z in groups:
                a.wait_ge(forget_ready, tally.due(forget_ready))
                a.wait_ge(input_gate_ready, tally.due(input_gate_ready))
                a.activation(z, z, ACT.Ln).then_inc(log_forget_ready, 1)
                a.wait_ge(log_forget_ready, tally.gave(log_forget_ready))
            for i in range(4):
                tag = ("hgc", i // 2, i % 2)
                if i >= 2:
                    a.wait_ge(key_decayed, tally.due(key_decayed))
                a.wait_ge(bank_filled[bank_of(tag)], nth(tag))
                ins = a.activation(R(WP + i % 2 * HALF, HALF), result(tag), ACT.Exp)
                ins.then_inc(bank_drained[bank_of(tag)], 1)
                a.wait_ge(bank_drained[bank_of(tag)], nth(tag))
            a.wait_ge(bank_filled[bank_of("decay")], nth("decay"))
            a.activation(sm(128, 64), result("decay")[:, 0:64], ACT.Exp).then_inc(bank_drained[bank_of("decay")], 1)
            a.wait_ge(bank_drained[bank_of("decay")], nth("decay"))
            a.wait_ge(key_decayed, tally.due(key_decayed, 2))
            for i in range(4):
                d, t = divmod(i, 2)
                if i >= 2:
                    a.wait_ge(query_key_decayed, tally.due(query_key_decayed))
                tag = ("hg", "pre32", d, t)
                a.wait_ge(bank_filled[bank_of(tag)], nth(tag))
                a.activation(R(BIAS + i * HALF, HALF), result(tag), ACT.Exp).then_inc(scalar_done, 1)
                a.wait_ge(scalar_done, tally.gave(scalar_done))
                a.wait_ge(bank_filled[bank_of(tag)], nth(tag))
                ins = a.activation(R(BIAS + 2048 + i * HALF, HALF), result(tag), ACT.Exp, scale=-1.0)
                ins.then_inc(bank_drained[bank_of(tag)], 1)
                a.wait_ge(bank_drained[bank_of(tag)], nth(tag))
                tag = ("hg", "suf32", d, t)
                a.wait_ge(bank_filled[bank_of(tag)], nth(tag))
                ins = a.activation(R(WP + i % 2 * HALF, HALF), result(tag), ACT.Exp)
                ins.then_inc(bank_drained[bank_of(tag)], 1)
                a.wait_ge(bank_drained[bank_of(tag)], nth(tag))
            a.wait_ge(query_key_decayed, tally.due(query_key_decayed, 2))
            for d in range(2):
                for t in range(TT):
                    for which, at in ((0, QDT), (1, KDT)):
                        tag = ("hgT", which, d, t)
                        a.wait_ge(bank_filled[bank_of(tag)], nth(tag))
                        ins = a.copy(R(at + (2 * d + t) * HALF, HALF), result(tag))
                        ins.then_inc(bank_drained[bank_of(tag)], 1)
                        a.wait_ge(bank_drained[bank_of(tag)], nth(tag))
            a.wait_ge(bank_drained[bank_of(("hgA", 1, 1))], nth(("hgA", 1, 1)))
            keep_rows("mod2_0", 1)

            def squares(o_tag, at):
                for t in range(TT):
                    a.wait_ge(bank_filled[bank_of((o_tag, t))], nth((o_tag, t)))
                    a.activation(R(at + t * HALF, HALF), result((o_tag, t)), ACT.Square).then_inc(squares_ready, 1)
                    a.wait_ge(squares_ready, tally.gave(squares_ready))
                root(sm(724, 8))

            squares("hgo", WP)
            mix_T("out1")
            sum_psum(JK2, lambda t, c: ("out1", c, t))
            a.wait_ge(x_ready, tally.due(x_ready, 2))
            normalise(lambda t: X[:, t, :], JK2, XN2)
            modulated_T("x2", 8, 24, 0, XT, 256, 0)
            a.wait_ge(bank_drained[bank_of("router")], nth("router"))
            a.activation(sm(0, 32), sm(0, 32), ACT.Exp).then_inc(affinity_exp, 1)
            a.wait_ge(affinity_exp, tally.gave(affinity_exp))
            for e in range(N_EXPERTS):
                for c in range(2):
                    tag = ("gu", e, 0, c)
                    if e:
                        a.wait_ge(bank_drained[bank_of(("gu", e - 1, 1, c))], nth(("gu", e - 1, 1, c)))
                    a.wait_ge(bank_filled[bank_of(tag)], nth(tag))
                    ins = a.activation(R(SG + c * GCH, GCH), result(tag)[:, 0:GCH], ACT.Silu)
                    ins.then_inc(bank_drained[bank_of(tag)], 1)
                    a.wait_ge(bank_drained[bank_of(tag)], nth(tag))
                if e:
                    a.wait_ge(bank_filled[bank_of(("comb", e - 1, 1, 1))], nth(("comb", e - 1, 1, 1)))
                for half in range(2):
                    tag = ("y", e, half)
                    a.wait_ge(bank_filled[bank_of(tag)], nth(tag))
                    a.copy(R(YS + half * HALF, HALF), result(tag)).then_inc(bank_drained[bank_of(tag)], 1)
                    a.wait_ge(bank_drained[bank_of(tag)], nth(tag))
            sum_rows(lambda t: R(ACC + t * D, D), JK2, lambda t, c: ("comb", N_EXPERTS - 1, t, c))
            a.wait_ge(x_ready, tally.due(x_ready, 2))
            normalise(lambda t: X[:, t, :], JK, XN)
            a.wait_ge(mod_cols_ready, tally.due(mod_cols_ready))
            modulated_T("x3", 0, 0, 0, XT, 512, 0)
            a.wait_ge(ctx_loaded, 16 * tally.due(ctx_loaded))
            normalise(lambda t: R(CX + t * D, D), JK, XN)
            modulated_T("ctx2", 16, 0, 1, XT, 512, 256)
            a.wait_ge(pads_zeroed, tally.due(pads_zeroed))
            for ff in range(14):
                if ff < 12:
                    tag = ("qkv", ff)
                    n = 1 if ff < 4 else 2
                    dst = R(CIN + ff % 2 * 2 * PADW, 2 * PADW).rearrange("p (s n) -> p s n", s=2)[:, 0:n, 2:2 + SEQ]
                    a.wait_ge(bank_filled[bank_of(tag)], nth(tag))
                    ins = a.copy(dst, result(tag).rearrange("p (s n) -> p s n", s=2)[:, 0:n, :])
                    ins.then_inc(bank_drained[bank_of(tag)], 1)
                    a.wait_ge(bank_drained[bank_of(tag)], nth(tag))
                if 1 <= ff <= 12:
                    f = ff - 1
                    a.wait_ge(short_conv_sum, tally.due(short_conv_sum))
                    co = R(COUT + f % 2 * HALF, SEQ if f < 4 else HALF)
                    a.activation(co, co, ACT.Silu).then_inc(short_conv_ready, 1)
                    a.wait_ge(short_conv_ready, tally.gave(short_conv_ready))
                if ff >= 2:
                    f = ff - 2
                    tag = ("qkvT", f)
                    a.wait_ge(bank_filled[bank_of(tag)], nth(tag))
                    ps = result(tag)
                    kind, h = divmod(f, 4)
                    base, tiles = ((QL, 2), (KL, 4), (VL, 4))[kind]
                    dst = R(base, tiles * HALF).rearrange("p (t n) -> p t n", t=tiles)[:, :, h * P:(h + 1) * P]
                    ins = a.copy(dst, ps.rearrange("p (t n) -> p t n", t=4)[:, 0:tiles, :])
                    ins.then_inc(bank_drained[bank_of(tag)], 1)
                    a.wait_ge(bank_drained[bank_of(tag)], nth(tag))
            root(sm(576, 24))
            root(sm(576, 16))
            root(sm(592, 8))
            for t in range(TT):
                dst = R(QBT, 1024).rearrange("p (i n) -> p i n", i=4)[:, :, t * P:(t + 1) * P]
                a.wait_ge(bank_filled[bank_of(("qbT", t))], nth(("qbT", t)))
                ins = a.copy(dst, result(("qbT", t)).rearrange("p (i n) -> p i n", i=4))
                ins.then_inc(bank_drained[bank_of(("qbT", t))], 1)
                a.wait_ge(bank_drained[bank_of(("qbT", t))], nth(("qbT", t)))
            for g in range(2):
                a.wait_ge(bank_filled[bank_of(("kbT", g))], nth(("kbT", g)))
                a.copy(R(KBT + g * HALF, HALF), result(("kbT", g))).then_inc(bank_drained[bank_of(("kbT", g))], 1)
                a.wait_ge(bank_drained[bank_of(("kbT", g))], nth(("kbT", g)))
            a.wait_ge(softplus_in, tally.due(softplus_in))
            a.activation(sm(160, 8), row("a_log"), ACT.Exp).then_inc(scalar_done, 1)
            a.wait_ge(scalar_done, tally.gave(scalar_done))
            a.activation(sm(96, 32), sm(96, 32), ACT.Exp).then_inc(softplus_exp, 1)
            a.wait_ge(softplus_exp, tally.gave(softplus_exp))
            a.wait_ge(softplus_one, tally.due(softplus_one))
            a.activation(sm(96, 32), sm(96, 32), ACT.Ln).then_inc(softplus_log, 1)
            a.wait_ge(softplus_log, tally.gave(softplus_log))
            attention("gq", WP2)
            ba = R(BKV, 4 * 272).rearrange("p (t n) -> p t n", t=4)
            ins = a.activation(sm(224, 32).rearrange("p (t n) -> p t n", t=4), ba[:, :, 0:8], ACT.Sigmoid)
            ins.then_inc(scalar_done, 1)
            a.wait_ge(scalar_done, tally.gave(scalar_done))
            for t in range(TT):
                z = R(ZG + t * HALF, HALF)
                a.activation(z, z, ACT.Silu).then_inc(delta_gate, 1)
                a.wait_ge(delta_gate, tally.gave(delta_gate))
            a.wait_ge(bank_filled[bank_of("gsums")], nth("gsums"))
            a.activation(sm(256, 96), result("gsums")[:, 0:96], ACT.Exp).then_inc(bank_drained[bank_of("gsums")], 1)
            a.wait_ge(bank_drained[bank_of("gsums")], nth("gsums"))
            a.wait_ge(bank_filled[bank_of("gsums1")], nth("gsums1"))
            ins = a.activation(sm(352, 32), result("gsums1")[:, 0:32], ACT.Exp)
            ins.then_inc(bank_drained[bank_of("gsums1")], 1)
            a.wait_ge(bank_drained[bank_of("gsums1")], nth("gsums1"))
            for seg, d in DELTA_PASSES:
                for t in range(TT):
                    tag = ("dec", seg, d, t)
                    a.wait_ge(bank_filled[bank_of(tag)], nth(tag))
                    ins = a.activation(R(DL + t * HALF, HALF), result(tag), ACT.Exp)
                    ins.then_inc(bank_drained[bank_of(tag)], 1)
                    a.wait_ge(bank_drained[bank_of(tag)], nth(tag))
                if seg == 0:
                    for t in range(TT):
                        tag = ("decT", d, t)
                        a.wait_ge(bank_filled[bank_of(tag)], nth(tag))
                        ins = a.activation(R(INT + t * HALF, HALF), result(tag), ACT.Exp)
                        ins.then_inc(bank_drained[bank_of(tag)], 1)
                        a.wait_ge(bank_drained[bank_of(tag)], nth(tag))
                for lv in range(1, N_LEVELS):
                    for t in range(TT):
                        tag = ("n1", seg, d, lv, t)
                        a.wait_ge(bank_filled[bank_of(tag)], nth(tag))
                        a.copy(R(DN + t * HALF, HALF), result(tag)).then_inc(bank_drained[bank_of(tag)], 1)
                        a.wait_ge(bank_drained[bank_of(tag)], nth(tag))
                for t in range(TT):
                    tag = ("w", seg, d, t)
                    a.wait_ge(bank_filled[bank_of(tag)], nth(tag))
                    a.copy(R(WW + t * HALF, HALF), result(tag)).then_inc(bank_drained[bank_of(tag)], 1)
                    a.wait_ge(bank_drained[bank_of(tag)], nth(tag))
                if seg == 1:
                    keep_rows("mod2_1", d)
            squares("dlo", DL)
            mix_T("out2")
            sum_psum(JKF, lambda t, c: ("out2", c, t))
            a.wait_ge(x_ready, tally.due(x_ready, 2))
            normalise(lambda t: X[:, t, :], JKF, YF)
            modulated_T("f0", 8, 24, 0, XT, 256, 0)
            ffn(0)
            sum_psum(JKF, lambda t, c: ("ffd0", t, c))
            a.wait_ge(x_ready, tally.due(x_ready, 2))
            normalise(lambda t: X[:, t, :], JKF, YF)
            a.wait_ge(mod_cols_ready, tally.due(mod_cols_ready))
            modulated_T("x4", 0, 0, 0, XT, 256, 0)
            for f in range(KT // 2):
                if f >= 2:
                    a.wait_ge(bank_drained[bank_of(("conf", f - 2, 0))], nth(("conf", f - 2, 0)))
                tag = ("conf", f, 1)
                a.wait_ge(bank_filled[bank_of(tag)], nth(tag))
                ps = result(tag)
                for i in range(2):
                    ins = a.activation(R(SGF + f % 2 * 512 + i * 256, 256), ps[:, i * 256:(i + 1) * 256], ACT.Sigmoid,
                                       bias=col("conf_b_in")[:, KT + 2 * f + i:KT + 2 * f + i + 1])
                    if i == 0:
                        ins.then_inc(scalar_done, 1)
                        a.wait_ge(scalar_done, tally.gave(scalar_done))
                    else:
                        ins.then_inc(bank_drained[bank_of(tag)], 1)
                        a.wait_ge(bank_drained[bank_of(tag)], nth(tag))
            a.wait_ge(bank_filled[bank_of("conv")], nth("conv"))
            ps = result("conv")
            for i in range(2):
                ft = KT - 2 + i
                ins = a.activation(R(CV + ft * 256, 256), ps[:, i * 256:(i + 1) * 256], ACT.Identity,
                                   bias=col("conf_dw_b")[:, ft:ft + 1])
                if i == 0:
                    ins.then_inc(scalar_done, 1)
                    a.wait_ge(scalar_done, tally.gave(scalar_done))
                else:
                    ins.then_inc(bank_drained[bank_of("conv")], 1)
                    a.wait_ge(bank_drained[bank_of("conv")], nth("conv"))
            a.wait_ge(centred_ready, tally.due(centred_ready))
            a.activation(R(SQ, 2048), R(CV, 2048), ACT.Square).then_inc(conf_var_in, 1)
            a.wait_ge(conf_var_in, tally.gave(conf_var_in))
            a.wait_ge(bank_drained[bank_of(("conf", "var"))], nth(("conf", "var")))
            a.activation(R(MU + 256, 256), R(MU + 256, 256), ACT.Sqrt).then_inc(root_ready, 1)
            a.wait_ge(root_ready, tally.gave(root_ready))
            a.wait_ge(layer_norm_ready, tally.due(layer_norm_ready))
            for f in range(KT):
                c = R(CV + f * 256, 256)
                ins = a.activation(c, c, ACT.Silu, scale=col("ln_g")[:, f:f + 1], bias=col("ln_b")[:, f:f + 1])
                ins.then_inc(conv_out_ready, 1)
                a.wait_ge(conv_out_ready, tally.gave(conv_out_ready))
            sum_rows(lambda t: R(YF + t * D, D), JKF, lambda t, c: ("confo", c, t))
            a.wait_ge(x_ready, tally.due(x_ready, 2))
            normalise(lambda t: X[:, t, :], JKF, YF)
            modulated_T("f1", 8, 24, 0, XT, 256, 0)
            ffn(1)
            sum_psum(JKF, lambda t, c: ("ffd1", t, c))

        @block.gpsimd
        def _(g):
            tally = Tally()
            g.wait_ge(bias_loaded, 16 * tally.due(bias_loaded))
            b3 = R(BIAS, 4096).rearrange("p (a k) -> p a k", k=64)
            ins = g.tensor_tensor(b3, b3, const("window").unsqueeze(1).to_broadcast([P, 64, 64]), ALU.add)
            ins.then_inc(bias_ready, 1)
            g.wait_ge(bias_ready, tally.gave(bias_ready))
            for z_at, k_at in GATES:
                g.wait_ge(forget_ready, tally.due(forget_ready))
                ins = g.tensor_tensor(R(k_at, HALF).rearrange("p (h e) -> p h e", h=4),
                                      const("ones").unsqueeze(1).to_broadcast([P, 4, P]),
                                      R(z_at, HALF).rearrange("p (h e) -> p h e", h=4), ALU.subtract)
                ins.then_inc(input_gate_ready, 1)
                g.wait_ge(input_gate_ready, tally.gave(input_gate_ready))
            for i in range(4):
                if i == 0:
                    g.wait_ge(bank_filled[bank_of("decay")], nth("decay"))
                g.memset(R(PC + 2 * D + i * HALF, HALF), 0.0).then_inc(intra_zeroed, 1)
                g.wait_ge(intra_zeroed, tally.gave(intra_zeroed))
            def h3(at):
                return R(at, HALF).rearrange("p (h e) -> p h e", h=4)

            def per_head(at):
                return sm(at, 4).unsqueeze(2).to_broadcast([P, 4, P])

            for seg, d in DELTA_PASSES:
                for lv in range(N_LEVELS):
                    for t in range(TT):
                        if lv == 0:
                            g.wait_ge(bank_drained[bank_of(("gram", seg, d, t))], nth(("gram", seg, d, t)))
                            if seg == 0:
                                g.wait_ge(bank_filled[bank_of(("decT", d, t))], nth(("decT", d, t)))
                        else:
                            g.wait_ge(bank_filled[bank_of(("n1", seg, d, lv - 1, t))],
                                      nth(("n1", seg, d, lv - 1, t)))
                            if lv == 1:
                                g.wait_ge(bank_drained[bank_of(("n1", seg, d, 0, t))], nth(("n1", seg, d, 0, t)))
                        mask = const(f"level{lv}_{d}").unsqueeze(1).to_broadcast([P, 4, P])
                        ins = g.tensor_tensor(h3(DC + t * HALF), h3(DL + t * HALF), mask, ALU.mult)
                        ins.then_inc(coupling_ready, 1)
                        g.wait_ge(coupling_ready, tally.gave(coupling_ready))
                    for t in range(TT):
                        at = (seg * 2 + t) * 8 + d * 4
                        k3, v3 = h3(KL + (seg * 2 + t) * HALF), h3(VL + (seg * 2 + t) * HALF)
                        if lv == 1:
                            g.wait_ge(bank_drained[bank_of("gsums")], nth("gsums"))
                            ins = g.tensor_tensor(h3(VBG + t * HALF), v3, per_head(224 + at), ALU.mult)
                            ins.then_inc(pool_done, 1)
                            g.wait_ge(pool_done, tally.gave(pool_done))
                        elif lv == 2:
                            ins = g.tensor_tensor(h3(KBG + t * HALF), k3, per_head(224 + at), ALU.mult)
                            ins.then_inc(pool_done, 1)
                            g.wait_ge(pool_done, tally.gave(pool_done))
                        elif lv == 3:
                            ins = g.tensor_tensor(h3(KBG + t * HALF), h3(KBG + t * HALF), per_head(256 + at),
                                                  ALU.mult)
                            ins.then_inc(pool_done, 1)
                            g.wait_ge(pool_done, tally.gave(pool_done))
                        elif lv == 4:
                            ins = g.tensor_tensor(h3(KTL + t * HALF), k3, per_head(288 + at), ALU.mult)
                            ins.then_inc(kv_scaled, 1)
                            g.wait_ge(kv_scaled, tally.gave(kv_scaled))

            g.wait_ge(bank_drained[bank_of(("mod2_1", "gate", 1, 1))], nth(("mod2_1", "gate", 1, 1)))
            for n in range(2 * CONF_K):
                if n >= N_DIAGS:
                    g.wait_ge(diag_used, tally.due(diag_used))
                at = (KT - 2) * CONF_K + n
                ins = g.tensor_tensor(diagonal(n), const("ident"),
                                      col("conf_dw_w")[:, at:at + 1].to_broadcast([P, P]), ALU.mult)
                ins.then_inc(diag_ready, 1)
                g.wait_ge(diag_ready, tally.gave(diag_ready))

        @block.sync
        def _(s):
            tally = Tally()
            def load(dst, src, tag):
                s.dma_start(dst, src).then_inc(tag, 16)

            by_order = list(order)

            def weights_in(key, *parts):
                n = order[key]
                if n >= RING:
                    freed, times = freed_by[by_order[n - RING]]
                    s.wait_ge(freed, times)
                for src, view in parts:
                    s.dma_start(view(slot(n % RING)), src).then_inc(slot_loaded[n % RING], 16)

            def mod_in(tag, w, k0, k1):
                for k in range(k0, k1):
                    for h in range(2):
                        src = w[k * P:(k + 1) * P, :].rearrange("p (j h n) -> p j h n", j=4, h=2)[:, :, h, :]
                        weights_in((tag, k, h), (src, lambda s: s.rearrange("p (j n) -> p j n", j=4)))

            def late_mod_in(tag, w, h):
                for k in range(KT):
                    src = w[k * P:(k + 1) * P, :].rearrange("p (j h n) -> p j h n", j=4, h=2)[:, :, h, :]
                    weights_in((tag, h, k), (src, lambda s: s.rearrange("p (j n) -> p j n", j=4)))

            def proj_in(tag, w, at, n, key):
                for h in range(2):
                    src = w[h * 512:(h + 1) * 512, at:at + n].rearrange("(k p) n -> p k n", p=P)
                    weights_in((tag, key, h), (src, lambda s: s[:, 0:4 * n].rearrange("p (k n) -> p k n", k=4)))

            def pair_in(tag, w, second, pairs):
                for f in range(pairs):
                    for h in range(2):
                        parts = []
                        for u in range(2):
                            src = w[h * 512:(h + 1) * 512, u * second + f * 256:u * second + (f + 1) * 256]
                            parts.append((src.rearrange("(k p) n -> p k n", p=P),
                                          lambda s, u=u: s[:, 0:2048].rearrange("p (k u n) -> p k u n", k=4, u=2)[:, :, u, :]))
                        weights_in((tag, f, h), *parts)

            def down_in(tag, w):
                for i in range((FT + 2) // 3):
                    n = min(3, FT - 3 * i)
                    src = w[i * 384:i * 384 + n * P, :].rearrange("(k p) n -> p k n", p=P)
                    weights_in((tag, i), (src, lambda s, n=n: s[:, 0:n * D].rearrange("p (k n) -> p k n", k=n)))

            def biases(b, at):
                s.wait_ge(mod_bias_zeroed, tally.due(mod_bias_zeroed))
                for i in range(2):
                    load(R(at, MODQ)[i:P:32, :], b.rearrange("(j n) -> j n", j=4), mod_bias_loaded)

            def post_rows(a, b):
                load(R(PR, D), a.partition_broadcast(P), post_gains_loaded)
                load(R(PR2, D), b.partition_broadcast(P), post_gains_loaded)

            def rows_in(dst, src, tag):
                load(dst.rearrange("p (t n) -> p t n", t=TT), src.rearrange("(t p) n -> p t n", p=P), tag)

            load(cols[:, :], T["cols"], cols_loaded)
            mod_in("mod1", T["w_mod"], 0, 4)
            load(consts[:, :], T["consts"], consts_loaded)
            biases(T["b_mod"], MB)
            mod_in("mod1", T["w_mod"], 4, 5)
            rows_in(x[:, :], T["x"], x_loaded)
            load(rows[:, :], T["rows"].partition_broadcast(P), rows_loaded)
            mod_in("mod1", T["w_mod"], 5, 6)
            rows_in(R(CX, 2048), T["ctx"], ctx_loaded)
            mod_in("mod1", T["w_mod"], 6, 7)
            post_rows(T["g_post1"], T["g_post2"])
            mod_in("mod1", T["w_mod"], 7, KT)
            for c in range(3):
                proj_in("in1", T["w_in"], c * 512, 512, c)
            s.wait_ge(bank_drained[bank_of(("mod1", "gate", 1, 1))], nth(("mod1", "gate", 1, 1)))
            rows_in(R(BIAS, 4096), T["bias"], bias_loaded)
            for c in range(3, 8):
                proj_in("in1", T["w_in"], c * 512, 512, c)
            late_mod_in("mod2_0", T["w_mod_2"][0], 0)
            late_mod_in("mod2_0", T["w_mod_2"][0], 1)
            for c in range(2):
                proj_in("out1", T["w_out"], c * 512, 512, c)
            for e in range(N_EXPERTS):
                if e == 1:
                    biases(T["b_mod_2"][0], XT)
                for k in range(KT):
                    for u, name in enumerate(("w_gate", "w_up")):
                        weights_in(("expert", e, u, k), (T[name][e, k * P:(k + 1) * P, :], lambda s: s[:, 0:D_EXPERT]))
                for half in range(2):
                    for j in range(4):
                        blk = T["w_down"][e, j * COLG:(j + 1) * COLG, half * HALF:(half + 1) * HALF]
                        weights_in(("down", e, half, j),
                                   (blk[0:QMAIN * P, :].rearrange("(p q) n -> p q n", q=QMAIN),
                                    lambda s: s.rearrange("p (q n) -> p q n", q=6)[:, 0:QMAIN, :]),
                                   (blk[QMAIN * P:COLG, :],
                                    lambda s: s[0:TAIL].rearrange("p (q n) -> p q n", q=6)[:, QMAIN, :]))
            for i in range(4):
                weights_in(("qkv", i), (T["hyb_w"][:, i * 384:(i + 1) * 384].rearrange("(k p) n -> p k n", p=P),
                                        lambda s: s.rearrange("p (k n) -> p k n", k=KT)))
            proj_in("hyb", T["hyb_w"], 1536, 512, "z")
            s.wait_ge(x_ready, tally.due(x_ready, 4))
            rows_in(R(CX, 2048), T["ctx_2"], ctx_loaded)
            post_rows(T["g_mix_post"][0], T["g_ffn_post"][0])
            proj_in("hyb", T["hyb_w"], 2064, 512, "q")
            weights_in(("hyb", "bkv"),
                       (T["hyb_w"][:, 2048:2064].rearrange("(k p) n -> p k n", p=P),
                        lambda s: s[:, 0:2176].rearrange("p (k n) -> p k n", k=KT)[:, :, 0:16]),
                       (T["hyb_w"][:, 2576:2832].rearrange("(k p) n -> p k n", p=P),
                        lambda s: s[:, 0:2176].rearrange("p (k n) -> p k n", k=KT)[:, :, 16:272]))
            for h in range(2):
                late_mod_in("mod2_1", T["w_mod_2"][1], h)
            for c in range(2):
                proj_in("out2", T["hyb_w_out"], c * 512, 512, c)
            pair_in("ffn0", T["w_ffn_in"][0], FFN, FT // 2)
            biases(T["b_mod_2"][1], MB)
            post_rows(T["g_mix_post"][1], T["g_ffn_post"][1])
            load(R(E0 + 4096, D), T["conf_b_out"].partition_broadcast(P), out_bias_loaded)
            down_in("ffd0", T["w_ffn_out"][0])
            pair_in("conf", T["conf_w_in"], D, KT // 2)
            for c in range(2):
                proj_in("confo", T["conf_w_out"], c * 512, 512, c)
            pair_in("ffn1", T["w_ffn_in"][1], FFN, FT // 2)
            down_in("ffd1", T["w_ffn_out"][1])
            s.wait_ge(out_ready, tally.due(out_ready, 2))
            s.dma_start(out.rearrange("(t p) n -> p t n", p=P), X).then_inc(stored, 16)
            s.wait_ge(stored, 16)

def kernel(**inputs):
    import concourse.bacc as bacc
    from concourse.bass_utils import run_bass_kernel_spmd

    arrays = layout(inputs)
    nc = bacc.Bacc("TRN2", target_bir_lowering=False, num_devices=1)
    T = {name: nc.dram_tensor(name + "_dram", a.shape, mybir.dt.from_np(a.dtype), kind="ExternalInput").ap()
         for name, a in arrays.items()}
    out = nc.dram_tensor("out_dram", (SEQ, D), F32, kind="ExternalOutput").ap()
    program(nc, T, out)
    r = run_bass_kernel_spmd(nc, [{name + "_dram": a for name, a in arrays.items()}], core_ids=[0])
    return r.results[0]["out_dram"].reshape(1, SEQ, D)


def layout(i):
    i = {k: np.ascontiguousarray(v) for k, v in i.items()}

    def columns(v):
        return v.reshape(-1, P).T

    def cond(c, c_ctx):
        z = np.zeros((P, KT, 32), np.float32)
        z[:, :, 0], z[:, :, 1] = columns(c.reshape(-1)), columns(c_ctx)
        return z.reshape(P, -1)

    parts = {
        "c1": cond(i["c"], i["c_ctx"]), "c2": cond(i["c_2"], i["c_ctx_2"]),
        "g_pre1": columns(i["g_pre1"][0]), "g_pre2": columns(i["g_pre2"][0]),
        "g_mix0": columns(i["g_mix_pre_2"][0]), "g_mix1": columns(i["g_mix_pre_2"][1]),
        "g_ffn0": columns(i["g_ffn_pre_2"][0]), "g_ffn1": columns(i["g_ffn_pre_2"][1]),
        "conf_b_in": columns(i["conf_b_in_2"][0]), "conf_dw_b": columns(i["conf_dw_b_2"][0]),
        "ln_g": columns(i["conf_ln_g_2"][0]), "ln_b": columns(i["conf_ln_b_2"][0]),
        "conf_dw_w": i["conf_dw_w_2"][0].reshape(CONF_K, KT, P).transpose(2, 1, 0).reshape(P, -1),
        "conv_w": i["hyb_conv_w_2"][0].reshape(SHORT_K, 12, P).transpose(2, 1, 0).reshape(P, -1),
        "w_router": i["w_router"][0].reshape(KT, P, N_EXPERTS).transpose(1, 0, 2).reshape(P, -1),
    }
    row_parts = {"hg_norm": i["hg_norm"][0], "logit0": i["hg_lb_logits"][0], "logit1": i["hg_lb_logits"][1],
                 "out_norm": i["hyb_out_norm_2"][0], "q_norm": i["hyb_q_norm_2"][0], "k_norm": i["hyb_k_norm_2"][0],
                 "a_log": i["hyb_a_log_2"].reshape(-1), "dt_bias": i["hyb_dt_bias_2"].reshape(-1)}
    tok = np.arange(SEQ)
    dr = tok[None, :] // 64 - tok[:, None] // 64 + 7
    dc = np.clip(tok[None, :] % 64 - tok[:, None] % 64 + 15, 0, 30)
    return {
        "cols": np.concatenate([parts[n] for n, _ in COLS], 1),
        "rows": np.concatenate([row_parts[n] for n, _ in ROWS]),
        "consts": CONSTS,
        "bias": i["na_rpb"][0][:, dr, dc].transpose(1, 0, 2).reshape(SEQ, -1),
        "x": i["x"][0], "ctx": i["ctx"][0], "ctx_2": i["ctx_2"][0],
        "w_mod": i["w_mod"][0], "b_mod": i["b_mod"][0], "g_post1": i["g_post1"][0], "g_post2": i["g_post2"][0],
        "w_in": i["w_in"][0], "w_out": i["w_out"][0],
        "w_gate": i["w_gate"][0], "w_up": i["w_up"][0], "w_down": i["w_down"][0],
        "w_mod_2": i["w_mod_2"], "b_mod_2": i["b_mod_2"], "g_mix_post": i["g_mix_post_2"],
        "g_ffn_post": i["g_ffn_post_2"], "w_ffn_in": i["w_ffn_in_2"], "w_ffn_out": i["w_ffn_out_2"],
        "hyb_w": i["hyb_w_in_2"][0], "hyb_w_out": i["hyb_w_out_2"][0],
        "conf_w_in": i["conf_w_in_2"][0], "conf_w_out": i["conf_w_out_2"][0], "conf_b_out": i["conf_b_out_2"][0],
    }
```
